# Optimizing a Trainium2 kernel written in Bass

```python
import jax, jax.numpy as jnp
from jax import lax
import numpy as np

D_MODEL = 1024
BATCH = 1
SEQ = 2048
DEPTH = 1

CHUNK = 64
GM_BLOCK = 128
GM_HEADS = 4
GM_HEAD_DIM = 128
GM_DIM = GM_HEADS * GM_HEAD_DIM
HG_HEADS = 4
HG_DK = 128
HG_DV = 128
HG_FDIM = HG_HEADS * HG_DK
HG_IDIM = HG_HEADS * HG_DV
N_BRANCH = 2
D_FF = 2816
CONV_W = 3
EPS = 1e-6
TINY = 1e-30
LB_MAX = 0.999
IN_SIZES = (GM_DIM, GM_DIM, HG_FDIM, HG_FDIM, HG_IDIM, HG_IDIM, N_BRANCH * D_MODEL)
IN_COLS = 2 * GM_DIM + 2 * HG_FDIM + 2 * HG_IDIM + N_BRANCH * D_MODEL

kernel_name = "hybrid_gmlp_hgrn2_convffn_trunk"

def _split_cols(z, sizes):
    outs, start = [], 0
    for s in sizes:
        outs.append(z[..., start:start + s])
        start += s
    return outs

def _rmsnorm(x, g):
    xf = x.astype(jnp.float32)
    r = lax.rsqrt(jnp.mean(xf * xf, axis=-1, keepdims=True) + EPS)
    return (xf * r).astype(x.dtype) * g

def _layernorm(x, g, b):
    xf = x.astype(jnp.float32)
    mu = jnp.mean(xf, axis=-1, keepdims=True)
    var = jnp.mean(jnp.square(xf - mu), axis=-1, keepdims=True)
    return ((xf - mu) * lax.rsqrt(var + EPS)).astype(x.dtype) * g + b

def _gmlp_branch(u, v, ln_g, ln_b, ws, bs):
    B, S, _ = v.shape
    nb = S // GM_BLOCK
    v = _layernorm(v, ln_g, ln_b)
    vb = v.reshape(B, nb, GM_BLOCK, GM_HEADS, GM_HEAD_DIM)
    pos = jnp.arange(GM_BLOCK) // CHUNK
    mask = pos[:, None] >= pos[None, :]
    w = jnp.where(mask[None], ws, 0.0).astype(v.dtype)
    mixed = jnp.einsum('hij,bnjhd->bnihd', w, vb) + bs.T[None, None, :, :, None]
    return u * mixed.reshape(B, S, GM_DIM)

def _hgrn2_chunk_step(state, inp):
    q, k, g, v = inp
    C = q.shape[2]
    G = jnp.cumsum(g, axis=2)
    causal = jnp.tril(jnp.ones((C, C), dtype=bool))[None, None, :, :, None]
    diff = G[:, :, :, None, :] - G[:, :, None, :, :]
    decay = jnp.where(causal, jnp.exp(jnp.minimum(diff, 0.0)), 0.0)
    A = jnp.einsum('bhid,bhijd,bhjd->bhij', q, decay, k)
    o = jnp.einsum('bhij,bhje->bhie', A, v) + jnp.einsum('bhid,bhde->bhie', q * jnp.exp(G), state)
    G_last = G[:, :, -1:, :]
    state = jnp.exp(G_last[:, :, 0, :])[..., None] * state + \
        jnp.einsum('bhjd,bhje->bhde', k * jnp.exp(G_last - G), v)
    return state, o

def _hgrn2_branch(q, f, i, og, lb, norm_g):
    B, S, _ = q.shape
    nc = S // CHUNK
    out_dtype = i.dtype
    qf = jax.nn.silu(q.astype(jnp.float32))
    ff = f.astype(jnp.float32)
    lb = jnp.clip(lb.astype(jnp.float32), 0.0, LB_MAX)
    forget = lb + (1.0 - lb) * jax.nn.sigmoid(ff)
    g_log = jnp.log(jnp.maximum(forget, TINY))
    k = (1.0 - lb) * jax.nn.sigmoid(-ff)
    vf = i.astype(jnp.float32)

    def to_chunks(t, d):
        return t.reshape(B, nc, CHUNK, HG_HEADS, d).transpose(1, 0, 3, 2, 4)

    xs = (to_chunks(qf, HG_DK), to_chunks(k, HG_DK), to_chunks(g_log, HG_DK), to_chunks(vf, HG_DV))
    s0 = jnp.zeros((B, HG_HEADS, HG_DK, HG_DV), jnp.float32)
    _, o = lax.scan(_hgrn2_chunk_step, s0, xs)
    o = o.transpose(1, 0, 3, 2, 4).reshape(B, S, HG_HEADS, HG_DV).astype(out_dtype)
    o = _rmsnorm(o, norm_g) * jax.nn.silu(og.reshape(B, S, HG_HEADS, HG_DV))
    return o.reshape(B, S, HG_IDIM)

def _conv_ffn(h, w_up, conv_w, conv_b, w_down):
    S = h.shape[1]
    z = h @ w_up
    zp = jnp.pad(z, ((0, 0), (CONV_W - 1, 0), (0, 0)))
    zc = conv_b + sum(zp[:, t:t + S, :] * conv_w[t] for t in range(CONV_W))
    gate, val = zc[..., :D_FF], zc[..., D_FF:]
    return (jax.nn.silu(gate) * val) @ w_down

def setup_inputs(seed: int = 0) -> dict:
    key = jax.random.key(seed)
    ks = jax.random.split(key, 20)
    f32 = jnp.float32

    def nrm(k, shape, scale):
        return jax.random.normal(k, shape, f32) * scale

    return {
        "x": nrm(ks[0], (BATCH, SEQ, D_MODEL), 1.0),
        "mix_norm": 1.0 + nrm(ks[1], (DEPTH, D_MODEL), 0.05),
        "w_in": nrm(ks[2], (DEPTH, D_MODEL, IN_COLS), D_MODEL ** -0.5),
        "gm_ln_g": 1.0 + nrm(ks[3], (DEPTH, GM_DIM), 0.05),
        "gm_ln_b": nrm(ks[4], (DEPTH, GM_DIM), 0.02),
        "gm_ws": nrm(ks[5], (DEPTH, GM_HEADS, GM_BLOCK, GM_BLOCK), GM_BLOCK ** -0.5),
        "gm_bs": 1.0 + nrm(ks[6], (DEPTH, GM_HEADS, GM_BLOCK), 0.1),
        "hg_lb_logits": nrm(ks[7], (DEPTH, HG_FDIM), 0.5),
        "hg_norm_g": 1.0 + nrm(ks[8], (DEPTH, HG_DV), 0.05),
        "w_br_gm": nrm(ks[9], (DEPTH, GM_DIM, D_MODEL), GM_DIM ** -0.5),
        "w_br_hg": nrm(ks[10], (DEPTH, HG_IDIM, D_MODEL), HG_IDIM ** -0.5),
        "w_out": nrm(ks[11], (DEPTH, D_MODEL, D_MODEL), D_MODEL ** -0.5),
        "ffn_norm": 1.0 + nrm(ks[12], (DEPTH, D_MODEL), 0.05),
        "w_up": nrm(ks[13], (DEPTH, D_MODEL, 2 * D_FF), D_MODEL ** -0.5),
        "conv_w": nrm(ks[14], (DEPTH, CONV_W, 2 * D_FF), CONV_W ** -0.5),
        "conv_b": nrm(ks[15], (DEPTH, 2 * D_FF), 0.02),
        "w_down": nrm(ks[16], (DEPTH, D_FF, D_MODEL), D_FF ** -0.5),
        "final_norm": 1.0 + nrm(ks[17], (D_MODEL,), 0.05),
    }

def reference(x, mix_norm, w_in, gm_ln_g, gm_ln_b, gm_ws, gm_bs, hg_lb_logits, hg_norm_g,
              w_br_gm, w_br_hg, w_out, ffn_norm, w_up, conv_w, conv_b, w_down, final_norm):
    p = jax.nn.softmax(hg_lb_logits.astype(jnp.float32), axis=0)
    lower_bounds = jnp.cumsum(p, axis=0) - p[0:1]
    for l in range(DEPTH):
        h = _rmsnorm(x, mix_norm[l])
        z = h @ w_in[l]
        u, v, q, f, i, og, gates = _split_cols(z, IN_SIZES)
        a = _gmlp_branch(jax.nn.gelu(u, approximate=False), jax.nn.gelu(v, approximate=False),
                         gm_ln_g[l], gm_ln_b[l], gm_ws[l], gm_bs[l])
        b = _hgrn2_branch(q, f, i, og, lower_bounds[l], hg_norm_g[l])
        gate_a, gate_b = gates[..., :D_MODEL], gates[..., D_MODEL:]
        y = jax.nn.sigmoid(gate_a) * (a @ w_br_gm[l]) + jax.nn.sigmoid(gate_b) * (b @ w_br_hg[l])
        x = x + y @ w_out[l]
        h = _rmsnorm(x, ffn_norm[l])
        x = x + _conv_ffn(h, w_up[l], conv_w[l], conv_b[l], w_down[l])
    return _rmsnorm(x, final_norm)


_drawn_inputs = setup_inputs


def setup_inputs(seed=0):
    import zlib

    import numpy as np

    out = dict(_drawn_inputs(seed))
    spreads = {}
    factors = {'gm_ln_g': 4.112,
     'gm_ln_b': 8.0,
     'hg_norm_g': 3.474,
     'conv_b': 4.232,
     'gm_bs': 2.955,
     'ffn_norm': 2.711}
    for name, (base, spread) in spreads.items():
        noise = np.random.default_rng([zlib.crc32(name.encode()), seed]).standard_normal(out[name].shape)
        drawn = base * np.exp(spread * noise) if base else spread * noise
        out[name] = __import__('jax').numpy.asarray(drawn.astype(out[name].dtype))
    for name, factor in factors.items():
        out[name] = (out[name] * factor).astype(out[name].dtype)
    return out
```

```python
import concourse.bass as bass
from concourse import mybir

F32 = mybir.dt.float32
F32R = mybir.dt.float32r
U32 = mybir.dt.uint32
ACT = mybir.ActivationFunctionType
ALU = mybir.AluOpType

P = 128
D = 1024
SEQ = 2048
TT = 512
NT = SEQ // TT
NC = TT // P
KD = D // P
NH = 4
FF = 2816
KF = FF // P
EPS = 1e-6
TINY = 1e-30
LB_MAX = 0.999
LEVELS = [1, 2, 4, 8, 16, 32, 64]
GM_CHUNK = 64
GM_BANKS = (2, 3, 5, 7)

U_FRONT = 0
U_MIX = U_FRONT + 6 * NH
U_OUT = U_MIX + 3 * KD
U_UP = U_OUT + KD
U_DOWN = U_UP + 2 * KF
UNITS = U_DOWN + 3 * KD
DOWN_SPLIT = [0, 8, 15, KF]
B_FRONT = 1
B_MIX = B_FRONT + 3 * NH
B_OUT = B_MIX + KD
B_UP = B_OUT + KD // 2
B_DOWN = B_UP + KF
B_TILE = B_DOWN + KD // 2 - B_FRONT

C_MIXN, C_FFNN, C_FINN = 0, KD, 2 * KD
C_LB = 3 * KD
C_LNG = C_LB + NH
C_HGN = C_LNG + NH
C_CW = C_HGN + 1
C_CB = C_CW + 3 * 2 * KF
N_PAR = C_CB + 2 * KF


class Steps:

    def __init__(self, sem, names, head_start=0):
        self.sem, self.names, self.n, self.head_start = sem, names, 0, head_start

    def did(self, name):
        assert self.names[self.n % len(self.names)] == name, (self.names[self.n % len(self.names)], name)
        self.n += 1
        return self.sem, 1

    def at(self, name, turn):
        return self.sem, turn * len(self.names) + (self.names.index(name) + 1 + self.head_start)

    def before(self, turn):
        return self.sem, turn * len(self.names) + self.head_start


def halves(ap, s):
    v = ap.rearrange("p (n two s) -> p n two s", two=2, s=s)
    return v[:, :, 0, :], v[:, :, 1, :]


def blocks(ap, s):
    return ap.rearrange("p (n s) -> p n s", s=s)


def spread(ap, s):
    return ap.unsqueeze(2).broadcast_to([P, ap.shape[1], s])


def build(nc, x_t, w_units, par, masks_in, ident_in, gm_wt, ln_b, gm_bs, out):
    top = [nc.sbuf_base + (-nc.sbuf_base) % 64]

    def place(name, shape, dt=F32, at=None):
        size = 4
        for n in shape[1:]:
            size *= n
        if at is None:
            at = top[0]
            top[0] += size + (-size) % 64
            assert top[0] <= nc.sbuf_usable_end, (name, top[0])
        return nc.alloc_sbuf_tensor_at(name, shape, dt, offset=at)

    def room(size):
        at = top[0]
        top[0] += size
        return at

    BLK = TT * 4
    raw = [place(f"raw{i}", [P, KD, P]) for i in range(2)]
    w_hi = [place(f"w_hi{i}", [P, KD, P], F32R) for i in range(2)]
    w_lo = [place(f"w_lo{i}", [P, KD, P], F32R) for i in range(2)]
    h_hi = place("h_hi", [P, KD, TT], F32R)
    at_lo = room(KD * BLK)
    h_lo = place("h_lo", [P, KD, TT], F32R, at_lo)
    x_in = place("x_in", [P, KD, TT], F32, at_lo)
    res = place("res", [P, KD, TT])
    carry = place("carry", [P, NH, P])
    state = place("state", [P, NC, P])
    halo = place("halo", [P, (NT + 1) * 2 * KF, 2])
    params = place("params", [P, N_PAR])
    lower = place("lower", [P, 4, NH])
    masks = place("masks", [P, NC * P + len(LEVELS) * NC * P // 2], U32)
    ident = place("ident", [P, P])
    ones = place("ones", [P, P])
    eps = place("eps", [P, 1])
    scratch = place("scratch", [P, 8])
    gm_w = place("gm_w", [P, NH, P])
    gm_b = place("gm_b", [P, NH, P])
    stats = place("stats", [P, NC, 6])
    moments = place("moments", [P, NC, 2])
    spreads = place("spreads", [P, 2, NC])

    arena = room(2 * KF * BLK)
    g_hi = place("g_hi", [P, KF, TT], F32R, arena)
    g_lo = place("g_lo", [P, KF, TT], F32R, arena + KF * BLK)
    a_hi = place("a_hi", [P, NH, TT], F32R, arena)
    a_lo = place("a_lo", [P, NH, TT], F32R, arena + 4 * BLK)
    b_hi = place("b_hi", [P, NH, TT], F32R, arena + 8 * BLK)
    b_lo = place("b_lo", [P, NH, TT], F32R, arena + 12 * BLK)
    y_at = arena + 16 * BLK
    y_hi = place("y_hi", [P, KD, TT], F32R, y_at)
    y_lo = place("y_lo", [P, KD, TT], F32R, y_at + KD * BLK)
    q0 = place("q0", [P, TT], F32, y_at)
    qp = place("qp", [P, TT], F32, y_at + BLK)
    kp = {s: place(f"kp{s}", [P, TT], F32, y_at + (2 + n) * BLK)
          for n, s in enumerate(LEVELS + [P])}
    q_right = {s: place(f"qr{s}", [P, TT // 2], F32, y_at + 10 * BLK + n * BLK // 2)
               for n, s in enumerate(LEVELS)}
    t_at = y_at + 14 * BLK
    total = {}
    for s in LEVELS + [P]:
        total[s] = place(f"total{s}", [P, TT // s], F32, t_at)
        t_at += TT // s * 4
    assert t_at <= y_at + 16 * BLK
    u_act = place("u_act", [P, NH, TT], F32, y_at + 16 * BLK)
    v_tok = place("v_tok", [P, NC, NH * P], F32, y_at + 20 * BLK)
    late = y_at + 24 * BLK
    og_act = place("og_act", [P, TT], F32, late)
    i_tok = place("i_tok", [P, TT], F32, late + BLK)
    k_tok = place("k_tok", [P, TT], F32, late + 2 * BLK)
    scores = place("scores", [P, TT], F32, late + 3 * BLK)
    assert late + 4 * BLK <= arena + 2 * KF * BLK

    SLOT = BLK + 64
    pool = room(10 * SLOT)

    def temp(name, slot, width=TT):
        return place(name, [P, width], F32, pool + slot * SLOT)

    sig_f, sig_nf, sig_q, sig_og = (temp(n, i) for i, n in enumerate(("sig_f", "sig_nf", "sig_q", "sig_og")))
    i_raw, v_act, o_sq, o_rms = temp("i_raw", 4), temp("v_act", 5), temp("o_sq", 6), temp("o_rms", 7)
    o_unit, b_f32 = temp("o_unit", 8), temp("b_f32", 9)
    sq_n, sum_n, rms_n, inv_n = temp("sq_n", 0), temp("sum_n", 1), temp("rms_n", 2), temp("inv_n", 3)
    h_f32 = [temp("h_f32a", 4), temp("h_f32b", 5)]
    sq_r, rms_r, inv_r, sum_r = temp("sq_r", 6), temp("rms_r", 7), temp("inv_r", 8), temp("sum_r", 9)
    conv = [temp("conv0", 0), temp("conv1", 1)]
    silu, g_f32 = temp("silu", 2), temp("g_f32", 3)
    z = [temp("z0", 4, TT + 2), temp("z1", 5, TT + 2)]
    gate_a, gate_b = [temp("ga0", 0), temp("ga1", 1)], [temp("gb0", 2), temp("gb1", 3)]
    gm_mix, a_f32 = temp("gm_mix", 8), temp("a_f32", 9)
    br_b, br_a, y_f32 = temp("br_b", 4), temp("br_a", 5), temp("y_f32", 6)
    lnb_row, bs_row = temp("lnb_row", 0), temp("bs_row", 1)

    bank = [nc.alloc_psum_tensor(f"bank{i}", [P, TT], F32) for i in range(8)]

    def sem(name):
        return nc.alloc_semaphore(name)

    consts_in, x_next_in, res_in, out_sent = sem("consts_in"), sem("x_next_in"), sem("res_in"), sem("out_sent")
    raw_in = [sem("raw_in0"), sem("raw_in1")]
    hi_made, lo_made, unit_done = sem("hi_made"), sem("lo_made"), sem("unit_done")
    evac = [sem("evac0"), sem("evac1")]
    N_CONST = 16 * 6

    head_act = Steps(sem("head_act"), ["sig_f", "sig_q", "sig_og", "i_tok", "k_tok", "v_tok", "o_sq", "o_rms"])
    head_pe = Steps(sem("head_pe"), ["i_tok", "s1", "diag", "k_tok", "s64_32", "s16_8", "s4_2", "v_tok", "update",
                                     "o", "o_sum"])
    names = ["forget", "floor", "qp1"]
    for s in LEVELS:
        names += [f"qr{s}", f"qp{2 * s}", f"kl{2 * s}", f"kr{2 * s}", f"t{2 * s}"]
    head_dve = Steps(sem("head_dve"), ["k"] + names + ["m1", "m0", "m64", "m32", "m16", "m8", "m4", "m2", "st0", "st1",
                                                       "st2", "st3", "st4", "inv", "unit", "b", "b_hi", "b_lo"])
    gm_dve = Steps(sem("gm_dve"), [f"bn{c}" for c in range(NC)] + [f"ag{c}" for c in range(NC)] + ["inv"]
                   + [f"vn{c}" for c in range(NC)]
                   + [f"{n}{h}" for h in range(NH) for n in ("mix", "a", "a_hi", "a_lo")])
    gm_act = Steps(sem("gm_act"), ["std"])
    gm_pe = Steps(sem("gm_pe"), [f"mix{h}" for h in range(NH)])
    mix_dve = Steps(sem("mix_dve"), [f"{n}{j}" for j in range(2) for n in ("b", "a", "y", "y_hi", "y_lo")], 1)
    res_act = Steps(sem("res_act"), ["sq"])
    res_dve = Steps(sem("res_dve"), ["sum"], 1)
    zero_dve = Steps(sem("zero_dve"), ["scores", "sum_out", "sum_down", "sum_n"])
    norm_pe = Steps(sem("norm_pe"), ["ssq"])
    norm_act = Steps(sem("norm_act"), ["rms"] + [f"hi{c}" for c in range(KD)])
    pre_act = Steps(sem("pre_act"), ["sq"])
    pre_dve = Steps(sem("pre_dve"), ["sum"], 1)
    names = ["inv"]
    for a in range(0, KD, 4):
        names.append(f"f{a}")
        for c in range(a, a + 4):
            names += ([f"f{c + 1}"] if c + 1 < a + 4 else []) + [f"lo{c}"]
    norm_dve = Steps(sem("norm_dve"), names)
    up_act = Steps(sem("up_act"), ["silu"])
    up_dve = Steps(sem("up_dve"), ["c0", "d0", "e0", "c1", "d1", "e1", "g", "g_hi", "g_lo"], 1)
    fin_pe, fin_act = Steps(sem("fin_pe"), ["ssq"]), Steps(sem("fin_act"), ["rms"])
    fin_dve = Steps(sem("fin_dve"), ["inv"] + [f"o{c}" for c in range(KD)], 1)
    pro_dve, pro_act, pro_pe = sem("pro_dve"), sem("pro_act"), sem("pro_pe")

    def par_col(c, n=1):
        return params[:, c:c + n]

    def par_dyn(c, i):
        return params[:, bass.ds(c + i, 1)]

    mask_of, at = {0: masks[:, 0:TT]}, TT
    for s in LEVELS:
        mask_of[s] = masks[:, at:at + TT // 2]
        at += TT // 2
    level_place = {1: (3, 0), 64: (5, 0), 32: (5, 1), 16: (6, 0), 8: (6, 1), 4: (7, 0), 2: (7, 1)}

    def level_out(s):
        b, half = level_place[s]
        return bank[b][:, half * TT // 2:(half + 1) * TT // 2]

    block = nc.Block()
    block.__enter__()

    @block.sync
    def _(sp):
        def load(unit, slot):
            sp.dma_start(raw[slot][:, :, :], w_units[unit]).then_inc(raw_in[slot], 16)

        def stream(t, first, last):
            with sp.Fori(0, (last - first) // 2) as i:
                for j in range(2):
                    sp.wait_ge(lo_made, t * UNITS + i * 2 + (first + j + 1))
                    load(i * 2 + (first + j + 2), j)

        for a, b in ((params[:, :], par), (masks[:, :], masks_in), (ident[:, :], ident_in), (gm_w[:, :, :], gm_wt),
                     (lnb_row[:, :], ln_b.broadcast_to([P, NH * P])), (bs_row[:, :], gm_bs.broadcast_to([P, NH * P]))):
            sp.dma_start(a, b).then_inc(consts_in, 16)
        sp.dma_start(x_in[:, :, :], x_t[0]).then_inc(x_next_in, 16)
        load(0, 0)
        load(1, 1)
        with sp.Fori(0, NT) as t:
            stream(t, 0, 12)
            sp.wait_ge(*fin_dve.before(t))
            sp.wait_ge(pro_dve, 1)
            sp.dma_start(out[t], res[:, :, :]).then_inc(out_sent, 16)
            stream(t, 12, 24)
            sp.wait_ge(out_sent, t * 16 + 16)
            sp.dma_start(res[:, :, :], x_t[t]).then_inc(res_in, 16)
            stream(t, 24, U_DOWN + 4)
            sp.wait_ge(unit_done, t * UNITS + U_DOWN)
            sp.dma_start(x_in[:, :, :], x_t[t + 1]).then_inc(x_next_in, 16)
            stream(t, U_DOWN + 4, UNITS)
        sp.wait_ge(*fin_dve.before(NT))
        sp.dma_start(out[NT], res[:, :, :]).then_inc(out_sent, 16)
        sp.wait_ge(out_sent, 16 * (NT + 1))

    @block.gpsimd
    def _(po):
        with po.Fori(0, (NT * UNITS + 2) // 2) as i:
            for j in range(2):
                po.wait_ge(hi_made, i * 2 + (j + 1))
                po.tensor_tensor(w_lo[j][:, :, :], raw[j][:, :, :], w_hi[j][:, :, :].bitcast(F32),
                                 ALU.subtract).then_inc(lo_made, 1)

    @block.scalar
    def _(act):
        def weights_hi(t, u, i=0):
            slot = u % 2
            act.wait_ge(unit_done, t * UNITS + i + (u + 1))
            act.wait_ge(raw_in[slot], t * (8 * UNITS) + i * 8 + 16 * (u // 2 + 2))
            act.activation(w_hi[slot][:, :, :], raw[slot][:, :, :], ACT.Copy).then_inc(hi_made, 1)

        def pre_square(turn, c):
            act.wait_ge(x_next_in, turn * 16 + 16)
            act.wait_ge(*pre_dve.before(turn * KD + c))
            act.activation(sq_n[:, :], x_in[:, c, :], ACT.Square).then_inc(*pre_act.did("sq"))

        def norm_rms(turn):
            act.wait_ge(*norm_pe.at("ssq", turn))
            act.activation(rms_n[:, :], bank[2][:, :], ACT.Sqrt, bias=eps[:, 0:1],
                           scale=1.0 / D).then_inc(*norm_act.did("rms"))

        def norm_hi(turn, a, b):
            for c in range(a, b):
                act.wait_ge(*norm_dve.at(f"f{c}", turn))
                act.activation(h_hi[:, c, :], h_f32[c % 2][:, :], ACT.Copy).then_inc(*norm_act.did(f"hi{c}"))

        for j in range(2):
            act.sem_inc(evac[j], 1)
            act.wait_ge(raw_in[j], 16)
            act.activation(w_hi[j][:, :, :], raw[j][:, :, :], ACT.Copy).then_inc(hi_made, 1)
        act.wait_ge(pro_dve, 2)
        act.activation(lower[:, 1, :], lower[:, 0, :], ACT.Exp).then_inc(pro_act, 1)
        act.wait_ge(pro_pe, 1)
        for c in range(KD):
            pre_square(0, c)
        norm_rms(0)
        norm_hi(0, 0, KD)

        with act.Fori(0, NT) as t:
            with act.Fori(0, NH) as h:
                it = t * NH + h
                u = h * 6
                weights_hi(t, 0, u)
                act.activation(sig_f[:, :], bank[0][:, :], ACT.Sigmoid).then_inc(*head_act.did("sig_f"))
                act.activation(sig_nf[:, :], bank[0][:, :], ACT.Sigmoid, scale=-1.0).then_inc(evac[0], 1)
                weights_hi(t, 1, u)
                act.activation(sig_q[:, :], bank[1][:, :], ACT.Sigmoid).then_inc(*head_act.did("sig_q"))
                weights_hi(t, 2, u)
                act.activation(i_raw[:, :], bank[0][:, :], ACT.Copy).then_inc(evac[0], 1)
                weights_hi(t, 3, u)
                act.activation(sig_og[:, :], bank[1][:, :], ACT.Sigmoid).then_inc(*head_act.did("sig_og"))
                act.wait_ge(*head_pe.at("i_tok", it))
                act.activation(i_tok[:, :], bank[2][:, :], ACT.Copy).then_inc(*head_act.did("i_tok"))
                weights_hi(t, 4, u)
                act.activation(v_act[:, :], bank[0][:, :], ACT.Gelu).then_inc(evac[0], 1)
                act.wait_ge(*head_pe.at("k_tok", it))
                act.activation(k_tok[:, :], bank[2][:, :], ACT.Copy).then_inc(*head_act.did("k_tok"))
                weights_hi(t, 5, u)
                act.activation(u_act[:, h, :], bank[1][:, :], ACT.Gelu).then_inc(evac[1], 1)
                act.wait_ge(*head_pe.at("v_tok", it))
                act.activation(v_tok[:, :, bass.ts(h, P)], blocks(bank[3][:, :], P),
                               ACT.Copy).then_inc(*head_act.did("v_tok"))
                act.wait_ge(*head_pe.at("o", it))
                act.activation(o_sq[:, :], bank[4][:, :], ACT.Square).then_inc(*head_act.did("o_sq"))
                act.wait_ge(*head_pe.at("o_sum", it))
                act.activation(o_rms[:, :], bank[5][:, :], ACT.Sqrt, bias=eps[:, 0:1],
                               scale=1.0 / P).then_inc(*head_act.did("o_rms"))

            act.wait_ge(*gm_dve.at(f"ag{NC - 1}", t))
            act.activation(spreads[:, 0, :], moments[:, :, 1], ACT.Sqrt, bias=eps[:, 0:1]).then_inc(*gm_act.did("std"))

            def mix_pair(t, it, u):
                act.wait_ge(*mix_dve.before(it))
                for j in range(2):
                    weights_hi(t, U_MIX + 2 * j, u)
                    act.activation(gate_a[j][:, :], bank[0][:, :], ACT.Sigmoid).then_inc(evac[0], 1)
                    weights_hi(t, U_MIX + 2 * j + 1, u)
                    act.activation(gate_b[j][:, :], bank[1][:, :], ACT.Sigmoid).then_inc(evac[1], 1)
                for j in range(2):
                    weights_hi(t, U_MIX + 4 + j, u)

            with act.Fori(0, KD // 2) as p:
                mix_pair(t, t * (KD // 2) + p, p * 6)

            with act.Fori(0, KD // 2) as p:
                for j in range(2):
                    weights_hi(t, U_OUT + j, p * 2)
                    act.wait_ge(evac[j], t * B_TILE + p + (B_OUT + 1))
                    act.wait_ge(*res_dve.before(t * (2 * KD) + p * 2 + j))
                    act.activation(sq_r[:, :], res[:, p * 2 + j, :],
                                   ACT.Square).then_inc(*res_act.did("sq"))
            norm_rms(t * 2 + 1)
            norm_hi(t * 2 + 1, 0, KD)

            with act.Fori(0, KF) as f:
                it = t * KF + f
                act.wait_ge(*up_dve.before(it))
                for j in range(2):
                    weights_hi(t, U_UP + j, f * 2)
                    col = t * (2 * KF) + f + j * KF
                    act.activation(z[j][:, 0:2], halo[:, col, :], ACT.Copy)
                    act.activation(halo[:, col + 2 * KF, :], bank[j][:, TT - 2:TT], ACT.Copy)
                    act.activation(z[j][:, 2:TT + 2], bank[j][:, :], ACT.Copy).then_inc(evac[j], 1)
                act.wait_ge(*up_dve.at("e0", it))
                act.activation(silu[:, :], conv[0][:, :], ACT.Silu).then_inc(*up_act.did("silu"))

            for p in range(KD // 2):
                for j in range(2):
                    for part in range(3):
                        weights_hi(t, U_DOWN + 6 * p + 3 * j + part)
                        if p == 1 and part < 2:
                            for c in range(4 * j + 2 * part, 4 * j + 2 * part + 2):
                                pre_square(t + 1, c)
                        if p == 2 and j == 0 and part == 0:
                            norm_rms(t * 2 + 2)
                        if p >= 2 and j == 0 and part < 2:
                            norm_hi(t * 2 + 2, 4 * (p - 2) + 2 * part, 4 * (p - 2) + 2 * part + 2)
                    c = 2 * p + j
                    act.wait_ge(evac[j], t * B_TILE + (B_DOWN + p + 1))
                    act.wait_ge(*res_dve.before(t * (2 * KD) + KD + c))
                    act.activation(sq_r[:, :], res[:, c, :], ACT.Square).then_inc(*res_act.did("sq"))
            act.wait_ge(*fin_pe.at("ssq", t))
            act.activation(rms_r[:, :], bank[3][:, :], ACT.Sqrt, bias=eps[:, 0:1],
                           scale=1.0 / D).then_inc(*fin_act.did("rms"))

    @block.vector
    def _(dve):
        def pre_sum(turn, c):
            dve.wait_ge(*pre_act.at("sq", turn * KD + c))
            dve.tensor_tensor(sum_n[:, :], sum_n[:, :], sq_n[:, :], ALU.add).then_inc(*pre_dve.did("sum"))

        def norm_inv(turn):
            dve.wait_ge(*norm_act.at("rms", turn))
            dve.reciprocal(inv_n[:, :], rms_n[:, :]).then_inc(*norm_dve.did("inv"))

        def norm_parts(turn, src, col, a, b):
            def whole(c):
                dve.wait_ge(*norm_dve.at(f"lo{c - 2}" if c > 1 else "inv", turn))
                dve.scalar_tensor_tensor(out=h_f32[c % 2][:, :], in0=src[:, c, :], scalar=par_col(col + c),
                                         in1=inv_n[:, :], op0=ALU.mult, op1=ALU.mult).then_inc(*norm_dve.did(f"f{c}"))
            whole(a)
            for c in range(a, b):
                if c + 1 < b:
                    whole(c + 1)
                dve.wait_ge(*norm_act.at(f"hi{c}", turn))
                dve.tensor_tensor(h_lo[:, c, :], h_f32[c % 2][:, :], h_hi[:, c, :].bitcast(F32),
                                  ALU.subtract).then_inc(*norm_dve.did(f"lo{c}"))

        for steps in (mix_dve, res_dve, pre_dve, up_dve, fin_dve):
            dve.sem_inc(steps.sem, steps.head_start)
        dve.memset(res[:, :, :], 0.0).then_inc(pro_dve, 1)
        dve.memset(carry[:, :, :], 0.0)
        dve.memset(halo[:, 0:2 * KF, :], 0.0)
        dve.memset(ones[:, :], 1.0)
        dve.memset(eps[:, :], EPS)
        dve.wait_ge(consts_in, N_CONST)
        dve.memset(gm_w[GM_CHUNK:P, :, 0:GM_CHUNK], 0.0)
        lb = par_col(C_LB, NH)
        dve.tensor_tensor(lower[:, 0, :], lb, lb, ALU.subtract).then_inc(pro_dve, 1)
        dve.wait_ge(pro_act, 1)
        dve.reciprocal(lower[:, 2, :], lower[:, 1, :]).then_inc(pro_dve, 1)
        dve.wait_ge(pro_dve, 3)
        dve.tensor_tensor(lower[:, 3, :], lower[:, 1, :], lower[:, 2, :], ALU.mult).then_inc(pro_dve, 1)
        dve.wait_ge(pro_dve, 4)
        dve.tensor_tensor(lower[:, 1, :], lower[:, 3, :], lower[:, 3, :], ALU.subtract).then_inc(pro_dve, 1)
        dve.wait_ge(pro_dve, 5)
        dve.tensor_scalar(lower[:, 2, :], lower[:, 1, :], 0.0, LB_MAX, ALU.max, ALU.min).then_inc(pro_dve, 1)
        dve.wait_ge(pro_dve, 6)
        dve.tensor_scalar(lower[:, 3, :], lower[:, 2, :], -1.0, 1.0, ALU.mult, ALU.add).then_inc(pro_dve, 1)
        dve.wait_ge(pro_pe, 1)
        dve.tensor_tensor(gm_b[:, :, :], blocks(bank[3][:, :], P), blocks(bs_row[:, :], P), ALU.add).then_inc(pro_dve, 1)
        dve.wait_ge(pro_dve, 8)
        dve.memset(sum_n[:, :], 0.0).then_inc(pro_dve, 1)
        dve.wait_ge(pro_dve, 9)
        for c in range(KD):
            pre_sum(0, c)
        norm_inv(0)
        norm_parts(0, x_in, C_MIXN, 0, KD // 2)
        norm_parts(0, x_in, C_MIXN, KD // 2, KD)

        with dve.Fori(0, NT) as t:
            dve.memset(scores[:, :], 0.0).then_inc(*zero_dve.did("scores"))
            with dve.Fori(0, NH) as h:
                it = t * NH + h
                used = t * B_TILE + h * 3 + B_FRONT
                keep = lower[:, 3, bass.ds(h, 1)]

                def then(name):
                    dve.wait_ge(*head_dve.at(name, it))

                dve.wait_ge(evac[0], used + 1)
                dve.tensor_scalar(kp[1][:, :], sig_nf[:, :], keep, None, ALU.mult).then_inc(*head_dve.did("k"))
                dve.wait_ge(*head_act.at("sig_f", it))
                dve.tensor_scalar(total[1][:, :], sig_f[:, :], keep, lower[:, 2, bass.ds(h, 1)], ALU.mult,
                                  ALU.add).then_inc(*head_dve.did("forget"))
                then("forget")
                dve.tensor_scalar(total[1][:, :], total[1][:, :], TINY, None, ALU.max).then_inc(*head_dve.did("floor"))
                dve.wait_ge(*head_act.at("sig_q", it))
                dve.tensor_tensor(q0[:, :], sig_q[:, :], bank[1][:, :], ALU.mult).then_inc(evac[1], 1)
                then("floor")
                dve.wait_ge(evac[1], used + 1)
                dve.tensor_tensor(qp[:, :], q0[:, :], total[1][:, :], ALU.mult).then_inc(*head_dve.did("qp1"))
                for s in LEVELS:
                    then(f"t{s}" if s > 1 else "qp1")
                    q_l, q_r = halves(qp[:, :], s)
                    k_l, k_r = halves(kp[s][:, :], s)
                    k2_l, k2_r = halves(kp[2 * s][:, :], s)
                    t_l, t_r = halves(total[s][:, :], 1)
                    t_l, t_r = t_l[:, :, 0], t_r[:, :, 0]
                    dve.tensor_copy(blocks(q_right[s][:, :], s), q_r).then_inc(*head_dve.did(f"qr{s}"))
                    then(f"qr{s}")
                    dve.tensor_tensor(q_r, blocks(q_right[s][:, :], s), spread(t_l, s),
                                      ALU.mult).then_inc(*head_dve.did(f"qp{2 * s}"))
                    dve.tensor_tensor(k2_l, k_l, spread(t_r, s), ALU.mult).then_inc(*head_dve.did(f"kl{2 * s}"))
                    dve.tensor_copy(k2_r, k_r).then_inc(*head_dve.did(f"kr{2 * s}"))
                    dve.tensor_tensor(total[2 * s][:, :], t_l, t_r, ALU.mult).then_inc(*head_dve.did(f"t{2 * s}"))
                dve.wait_ge(*head_act.at("sig_og", it))
                dve.tensor_tensor(og_act[:, :], sig_og[:, :], bank[1][:, :], ALU.mult).then_inc(evac[1], 1)

                for n, (s, made, before) in enumerate(((1, "s1", f"t{P}"), (0, "diag", "m1"), (64, "s64_32", "m0"),
                                                       (32, "s64_32", "m64"), (16, "s16_8", "m32"),
                                                       (8, "s16_8", "m16"), (4, "s4_2", "m8"), (2, "s4_2", "m4"))):
                    dve.wait_ge(*zero_dve.at("scores", t))
                    dve.wait_ge(*head_pe.at(made, it))
                    then(before)
                    dve.memset(scratch[:, n:n + 1], 0.0)
                    if s:
                        dve.copy_predicated(halves(scores[:, :], s)[1], blocks(mask_of[s], s),
                                            blocks(level_out(s), s)).then_inc(*head_dve.did(f"m{s}"))
                    else:
                        dve.copy_predicated(scores[:, :], mask_of[0], bank[4][:, :]).then_inc(*head_dve.did("m0"))
                dve.tensor_copy(state[:, 0, :], carry[:, h, :]).then_inc(*head_dve.did("st0"))
                dve.wait_ge(*head_pe.at("update", it))
                for c in range(NC):
                    then(f"st{c}")
                    dve.scalar_tensor_tensor(out=state[:, c + 1, :] if c + 1 < NC else carry[:, h, :],
                                             in0=state[:, c, :], scalar=total[P][:, c:c + 1],
                                             in1=bank[2][:, c * P:(c + 1) * P], op0=ALU.mult,
                                             op1=ALU.add).then_inc(*head_dve.did(f"st{c + 1}"))
                dve.wait_ge(*head_act.at("o_rms", it))
                dve.reciprocal(o_rms[:, :], o_rms[:, :]).then_inc(*head_dve.did("inv"))
                then("inv")
                dve.tensor_tensor(o_unit[:, :], o_rms[:, :], bank[4][:, :], ALU.mult).then_inc(*head_dve.did("unit"))
                then("unit")
                dve.scalar_tensor_tensor(out=b_f32[:, :], in0=o_unit[:, :], scalar=par_col(C_HGN), in1=og_act[:, :],
                                         op0=ALU.mult, op1=ALU.mult).then_inc(*head_dve.did("b"))
                then("b")
                dve.tensor_scalar(b_hi[:, h, :], b_f32[:, :], 1.0, None, ALU.mult).then_inc(*head_dve.did("b_hi"))
                then("b_hi")
                dve.tensor_tensor(b_lo[:, h, :], b_f32[:, :], b_hi[:, h, :].bitcast(F32),
                                  ALU.subtract).then_inc(*head_dve.did("b_lo"))

            dve.wait_ge(*head_act.at("v_tok", t * NH + (NH - 1)))
            for c in range(NC):
                dve.bn_stats(out=stats[:, c, :], in_=v_tok[:, c, :]).then_inc(*gm_dve.did(f"bn{c}"))
            dve.wait_ge(*gm_dve.at(f"bn{NC - 1}", t))
            dve.memset(scratch[:, 0:1], 0.0)
            for c in range(NC):
                dve.bn_aggr(out=moments[:, c, :], in_=stats[:, c, :]).then_inc(*gm_dve.did(f"ag{c}"))
            dve.wait_ge(*gm_act.at("std", t))
            dve.reciprocal(spreads[:, 1, :], spreads[:, 0, :]).then_inc(*gm_dve.did("inv"))
            dve.wait_ge(*gm_dve.at("inv", t))
            for c in range(NC):
                dve.tensor_scalar(v_tok[:, c, :], v_tok[:, c, :], moments[:, c, 0:1], spreads[:, 1, c:c + 1],
                                  ALU.subtract, ALU.mult).then_inc(*gm_dve.did(f"vn{c}"))
            for h in range(NH):
                dve.wait_ge(*gm_pe.at(f"mix{h}", t))
                dve.scalar_tensor_tensor(out=blocks(gm_mix[:, :], P), in0=blocks(bank[GM_BANKS[h]][:, :], P),
                                         scalar=par_col(C_LNG + h),
                                         in1=gm_b[:, h, :].unsqueeze(1).broadcast_to([P, NC, P]),
                                         op0=ALU.mult, op1=ALU.add).then_inc(*gm_dve.did(f"mix{h}"))
                dve.wait_ge(*gm_dve.at(f"mix{h}", t))
                dve.tensor_tensor(a_f32[:, :], gm_mix[:, :], u_act[:, h, :], ALU.mult).then_inc(*gm_dve.did(f"a{h}"))
                dve.wait_ge(*gm_dve.at(f"a{h}", t))
                dve.tensor_copy(a_hi[:, h, :], a_f32[:, :]).then_inc(*gm_dve.did(f"a_hi{h}"))
                dve.wait_ge(*gm_dve.at(f"a_hi{h}", t))
                dve.tensor_tensor(a_lo[:, h, :], a_f32[:, :], a_hi[:, h, :].bitcast(F32),
                                  ALU.subtract).then_inc(*gm_dve.did(f"a_lo{h}"))

            with dve.Fori(0, KD // 2) as p:
                it = t * (KD // 2) + p

                def then(name):
                    dve.wait_ge(*mix_dve.at(name, it))

                for j in range(2):
                    dve.wait_ge(unit_done, t * UNITS + p * 6 + (U_MIX + 4 + j + 1))
                    dve.wait_ge(evac[1], t * B_TILE + p * 2 + (B_MIX + j + 1))
                    dve.tensor_tensor(br_b[:, :], gate_b[j][:, :], bank[4 + j][:, :],
                                      ALU.mult).then_inc(*mix_dve.did(f"b{j}"))
                    dve.tensor_tensor(br_a[:, :], gate_a[j][:, :], bank[6 + j][:, :],
                                      ALU.mult).then_inc(*mix_dve.did(f"a{j}"))
                    then(f"a{j}")
                    dve.tensor_tensor(y_f32[:, :], br_a[:, :], br_b[:, :], ALU.add).then_inc(*mix_dve.did(f"y{j}"))
                    then(f"y{j}")
                    block_c = p * 2 + j
                    dve.tensor_scalar(y_hi[:, block_c, :], y_f32[:, :], 1.0, None,
                                      ALU.mult).then_inc(*mix_dve.did(f"y_hi{j}"))
                    then(f"y_hi{j}")
                    dve.tensor_tensor(y_lo[:, block_c, :], y_f32[:, :], y_hi[:, block_c, :].bitcast(F32),
                                      ALU.subtract).then_inc(*mix_dve.did(f"y_lo{j}"))

            dve.memset(sum_r[:, :], 0.0).then_inc(*zero_dve.did("sum_out"))
            with dve.Fori(0, KD // 2) as p:
                dve.wait_ge(*zero_dve.at("sum_out", t))
                dve.wait_ge(res_in, t * 16 + 16)
                for j in range(2):
                    dve.wait_ge(unit_done, t * UNITS + p * 2 + (U_OUT + j + 1))
                    res_c = res[:, p * 2 + j, :]
                    dve.tensor_tensor(res_c, res_c, bank[j][:, :], ALU.add).then_inc(evac[j], 1)
                    dve.wait_ge(*res_act.at("sq", t * (2 * KD) + p * 2 + j))
                    dve.tensor_tensor(sum_r[:, :], sum_r[:, :], sq_r[:, :], ALU.add).then_inc(*res_dve.did("sum"))
            norm_inv(t * 2 + 1)
            norm_parts(t * 2 + 1, res, C_FFNN, 0, KD // 2)
            norm_parts(t * 2 + 1, res, C_FFNN, KD // 2, KD)

            with dve.Fori(0, KF) as f:
                it = t * KF + f

                def then(name):
                    dve.wait_ge(*up_dve.at(name, it))

                for j in range(2):
                    ch = f + j * KF
                    dve.wait_ge(evac[j], t * B_TILE + f + (B_UP + 1))
                    dve.tensor_scalar(conv[j][:, :], z[j][:, 2:TT + 2], par_dyn(C_CW + 4 * KF, ch), par_dyn(C_CB, ch),
                                      ALU.mult, ALU.add).then_inc(*up_dve.did(f"c{j}"))
                    for tap, name, before in ((1, "d", "c"), (0, "e", "d")):
                        then(f"{before}{j}")
                        dve.scalar_tensor_tensor(out=conv[j][:, :], in0=z[j][:, tap:TT + tap],
                                                 scalar=par_dyn(C_CW + 2 * KF * tap, ch), in1=conv[j][:, :],
                                                 op0=ALU.mult, op1=ALU.add).then_inc(*up_dve.did(f"{name}{j}"))
                dve.wait_ge(*up_act.at("silu", it))
                then("e1")
                dve.tensor_tensor(g_f32[:, :], silu[:, :], conv[1][:, :], ALU.mult).then_inc(*up_dve.did("g"))
                then("g")
                dve.tensor_scalar(g_hi[:, f, :], g_f32[:, :], 1.0, None, ALU.mult).then_inc(*up_dve.did("g_hi"))
                then("g_hi")
                dve.tensor_tensor(g_lo[:, f, :], g_f32[:, :], g_hi[:, f, :].bitcast(F32),
                                  ALU.subtract).then_inc(*up_dve.did("g_lo"))

            dve.memset(sum_r[:, :], 0.0).then_inc(*zero_dve.did("sum_down"))
            dve.memset(sum_n[:, :], 0.0).then_inc(*zero_dve.did("sum_n"))
            dve.wait_ge(*zero_dve.at("sum_n", t))
            for p in range(KD // 2):
                if p == 2:
                    norm_inv(t * 2 + 2)
                if p >= 2:
                    norm_parts(t * 2 + 2, x_in, C_MIXN, 4 * (p - 2), 4 * (p - 1))
                for j in range(2):
                    if p == 1:
                        for c in range(4 * j, 4 * j + 4):
                            pre_sum(t + 1, c)
                    c = 2 * p + j
                    dve.wait_ge(unit_done, t * UNITS + (U_DOWN + 3 * c + 3))
                    dve.tensor_tensor(res[:, c, :], res[:, c, :], bank[j][:, :], ALU.add).then_inc(evac[j], 1)
                    dve.wait_ge(*res_act.at("sq", t * (2 * KD) + KD + c))
                    dve.tensor_tensor(sum_r[:, :], sum_r[:, :], sq_r[:, :], ALU.add).then_inc(*res_dve.did("sum"))
            dve.wait_ge(*fin_act.at("rms", t))
            dve.reciprocal(inv_r[:, :], rms_r[:, :]).then_inc(*fin_dve.did("inv"))
            dve.wait_ge(*fin_dve.at("inv", t))
            for c in range(KD):
                dve.scalar_tensor_tensor(out=res[:, c, :], in0=res[:, c, :], scalar=par_col(C_FINN + c),
                                         in1=inv_r[:, :], op0=ALU.mult, op1=ALU.mult).then_inc(*fin_dve.did(f"o{c}"))

    @block.tensor
    def _(pe):
        def products(t, u, i, dst, rhs_hi, rhs_lo, n, first=True, last=True, off=0, ready=None, done=True):
            slot = u % 2
            if ready is None:
                pe.wait_ge(hi_made, t * UNITS + i + (u + 1))
                for k in range(n):
                    pe.matmul(dst, w_hi[slot][:, off + k, :], rhs_hi(k), start=first and k == 0, stop=False)
                    pe.matmul(dst, w_hi[slot][:, off + k, :], rhs_lo(k), start=False, stop=False)
                pe.wait_ge(lo_made, t * UNITS + i + (u + 1))
                for k in range(n):
                    mm = pe.matmul(dst, w_lo[slot][:, off + k, :], rhs_hi(k), start=False, stop=last and k == n - 1)
            else:
                pe.wait_ge(lo_made, t * UNITS + i + (u + 1))
                for k in range(n):
                    pe.wait_ge(*ready(k))
                    pe.matmul(dst, w_hi[slot][:, off + k, :], rhs_hi(k), start=first and k == 0, stop=False)
                    pe.matmul(dst, w_hi[slot][:, off + k, :], rhs_lo(k), start=False, stop=False)
                    mm = pe.matmul(dst, w_lo[slot][:, off + k, :], rhs_hi(k), start=False, stop=last and k == n - 1)
            if done:
                mm.then_inc(unit_done, 1)

        def from_h(t, u, i, b, uses, ready=None):
            pe.wait_ge(evac[b], uses)
            products(t, u, i, bank[b][:, :], lambda k: h_hi[:, k, :], lambda k: h_lo[:, k, :], KD, ready=ready)

        def norm_sum(turn):
            mm = pe.matmul(bank[2][:, :], ones[:, :], sum_n[:, :], start=True, stop=True)
            mm.then_inc(*norm_pe.did("ssq"))

        def flip(dst, src):
            for c in range(NC):
                mm = pe.transpose(dst[:, c * P:(c + 1) * P], src[:, c * P:(c + 1) * P], ident[:, :])
            return mm

        def level(s):
            dst = level_out(s)
            for c in range(NC):
                mm = pe.matmul(dst[:, c * P // 2:(c + 1) * P // 2], kp[s][:, c * P:(c + 1) * P],
                               q_right[s][:, c * P // 2:(c + 1) * P // 2], start=True, stop=True)
            return mm

        pe.wait_ge(consts_in, N_CONST)
        pe.wait_ge(pro_dve, 2)
        for h in range(NH):
            mm = pe.matmul(bank[3][:, h * P:(h + 1) * P], lnb_row[:, h * P:(h + 1) * P], gm_w[:, h, :],
                           start=True, stop=True)
        mm.then_inc(pro_pe, 1)
        pe.wait_ge(*pre_dve.at("sum", KD - 1))
        norm_sum(0)

        with pe.Fori(0, NT) as t:
            with pe.Fori(0, NH) as h:
                pe.wait_ge(*norm_dve.at(f"lo{KD - 1}", t * 2))
                it = t * NH + h
                u = h * 6
                used = t * B_TILE + h * 3 + B_FRONT
                from_h(t, 0, u, 0, used)
                from_h(t, 1, u, 1, used)
                from_h(t, 2, u, 0, used + 1)
                from_h(t, 3, u, 1, used + 1)
                pe.wait_ge(evac[0], used + 2)
                flip(bank[2], i_raw).then_inc(*head_pe.did("i_tok"))
                pe.wait_ge(*head_dve.at("qr1", it))
                level(1).then_inc(*head_pe.did("s1"))
                for c in range(NC):
                    cols = slice(c * P, (c + 1) * P)
                    mm = pe.matmul(bank[4][:, cols], kp[1][:, cols], q0[:, cols], start=True, stop=True)
                mm.then_inc(*head_pe.did("diag"))
                from_h(t, 4, u, 0, used + 2)
                pe.wait_ge(*head_act.at("i_tok", it))
                pe.wait_ge(*head_dve.at(f"t{P}", it))
                flip(bank[2], kp[P]).then_inc(*head_pe.did("k_tok"))
                for a, b in ((64, 32), (16, 8), (4, 2)):
                    level(a)
                    level(b).then_inc(*head_pe.did(f"s{a}_{b}"))
                from_h(t, 5, u, 1, used + 2)
                pe.wait_ge(evac[0], used + 3)
                pe.wait_ge(*head_dve.at("m2", it))
                flip(bank[3], v_act).then_inc(*head_pe.did("v_tok"))
                pe.wait_ge(*head_act.at("k_tok", it))
                for c in range(NC):
                    cols = slice(c * P, (c + 1) * P)
                    mm = pe.matmul(bank[2][:, cols], k_tok[:, cols], i_tok[:, cols], start=True, stop=True)
                mm.then_inc(*head_pe.did("update"))
                for c in range(NC):
                    cols = slice(c * P, (c + 1) * P)
                    pe.matmul(bank[4][:, cols], i_tok[:, cols], scores[:, cols], start=True, stop=False)
                    pe.wait_ge(*head_dve.at(f"st{c}", it))
                    mm = pe.matmul(bank[4][:, cols], state[:, c, :], qp[:, cols], start=False, stop=True)
                mm.then_inc(*head_pe.did("o"))
                pe.wait_ge(*head_act.at("o_sq", it))
                pe.wait_ge(*head_dve.at("st4", it))
                pe.matmul(bank[5][:, :], ones[:, :], o_sq[:, :], start=True,
                          stop=True).then_inc(*head_pe.did("o_sum"))

            def gates(u, used):
                for j in range(2):
                    from_h(t, U_MIX + 2 * j, u, 0, used + j)
                    from_h(t, U_MIX + 2 * j + 1, u, 1, used + j)

            def branches(u, it, a_ready=None):
                pe.wait_ge(*mix_dve.before(it))
                for j in range(2):
                    products(t, U_MIX + 4 + j, u, bank[4 + j][:, :], lambda k: b_hi[:, k, :],
                             lambda k: b_lo[:, k, :], NH, done=False)
                    products(t, U_MIX + 4 + j, u, bank[6 + j][:, :], lambda k: a_hi[:, k, :],
                             lambda k: a_lo[:, k, :], NH, off=NH, ready=a_ready if j == 0 else None)

            gates(0, t * B_TILE + B_MIX)
            pe.wait_ge(*gm_dve.at(f"vn{NC - 1}", t))
            for h in range(NH):
                for c in range(NC):
                    mm = pe.matmul(bank[GM_BANKS[h]][:, c * P:(c + 1) * P], v_tok[:, c, h * P:(h + 1) * P],
                                   gm_w[:, h, :], start=True, stop=True)
                mm.then_inc(*gm_pe.did(f"mix{h}"))
            pe.wait_ge(*head_dve.at("b_lo", t * NH + (NH - 1)))
            branches(0, t * (KD // 2), lambda k: gm_dve.at(f"a_lo{k}", t))
            with pe.Fori(1, KD // 2) as p:
                gates(p * 6, t * B_TILE + p * 2 + B_MIX)
                branches(p * 6, t * (KD // 2) + p)

            def project(i, uses, ready=None):
                for j in range(2):
                    pe.wait_ge(evac[j], uses)
                    products(t, U_OUT + j, i, bank[j][:, :], lambda k: y_hi[:, k, :], lambda k: y_lo[:, k, :], KD,
                             ready=ready if j == 0 else None)

            project(0, t * B_TILE + B_OUT, lambda k: mix_dve.at(f"y_lo{k % 2}", t * (KD // 2) + k // 2))
            with pe.Fori(1, KD // 2) as p:
                project(p * 2, t * B_TILE + p + B_OUT)
            pe.wait_ge(*res_dve.before(t * (2 * KD) + KD))
            pe.matmul(bank[2][:, :], ones[:, :], sum_r[:, :], start=True, stop=True).then_inc(*norm_pe.did("ssq"))

            ready = lambda k: norm_dve.at(f"lo{k}", t * 2 + 1)
            from_h(t, U_UP, 0, 0, t * B_TILE + B_UP, ready=ready)
            from_h(t, U_UP + 1, 0, 1, t * B_TILE + B_UP)
            with pe.Fori(1, KF) as f:
                for j in range(2):
                    from_h(t, U_UP + j, f * 2, j, t * B_TILE + f + B_UP)

            def down(c, i, ready=None):
                j = c % 2
                for part in range(3):
                    a, b = DOWN_SPLIT[part], DOWN_SPLIT[part + 1]
                    if part == 2 and ready:
                        pe.wait_ge(*ready)
                    products(t, U_DOWN + 3 * c + part, i, bank[j][:, :], lambda k: g_hi[:, a + k, :],
                             lambda k: g_lo[:, a + k, :], b - a, first=part == 0, last=part == 2)

            pe.wait_ge(*up_dve.at("g_lo", t * KF + (KF - 2)))
            for c in range(4):
                pe.wait_ge(evac[c % 2], t * B_TILE + (B_DOWN + c // 2))
                down(c, 0, up_dve.at("g_lo", t * KF + (KF - 1)) if c == 0 else None)
            pe.wait_ge(*pre_dve.before((t + 1) * KD + KD))
            norm_sum(t * 2 + 2)
            with pe.Fori(2, KD // 2) as p:
                for c in range(2):
                    pe.wait_ge(evac[c], t * B_TILE + p + B_DOWN)
                    down(c, p * 6)
            pe.wait_ge(*res_dve.before(t * (2 * KD) + 2 * KD))
            pe.matmul(bank[3][:, :], ones[:, :], sum_r[:, :], start=True, stop=True).then_inc(*fin_pe.did("ssq"))

    block.__exit__(None, None, None)


_ORDER = ("x_t", "w_units", "par", "masks_in", "ident_in", "gm_wt", "ln_b", "gm_bs")


def _columns(a):
    import numpy as np
    return np.asarray(a).reshape(-1, P).T


def _units(inputs):
    import numpy as np

    def unit(w, col, k0=0, k1=None):
        a = np.asarray(w)[k0 * P:None if k1 is None else k1 * P, col * P:(col + 1) * P]
        return a.reshape(-1, P, P).transpose(1, 0, 2)

    w_in, w_up, w_down = inputs["w_in"][0], inputs["w_up"][0], inputs["w_down"][0]
    u_at, v_at, q_at, f_at, i_at, og_at = (NH * n for n in range(6))
    ga_at, gb_at = 6 * NH, 6 * NH + KD
    out = np.zeros((UNITS + 2, P, KD, P), np.float32)
    n = 0
    for h in range(NH):
        for at in (f_at, q_at, i_at, og_at, v_at, u_at):
            out[n] = unit(w_in, at + h)
            n += 1
    for c in range(0, KD, 2):
        for at in (ga_at + c, gb_at + c, ga_at + c + 1, gb_at + c + 1):
            out[n] = unit(w_in, at)
            n += 1
        for j in range(2):
            out[n, :, :NH] = unit(inputs["w_br_hg"][0], c + j)
            out[n, :, NH:] = unit(inputs["w_br_gm"][0], c + j)
            n += 1
    for c in range(KD):
        out[n] = unit(inputs["w_out"][0], c)
        n += 1
    for f in range(KF):
        out[n], out[n + 1] = unit(w_up, f), unit(w_up, KF + f)
        n += 2
    for c in range(KD):
        for a, b in zip(DOWN_SPLIT, DOWN_SPLIT[1:]):
            out[n, :, :b - a] = unit(w_down, c, a, b)
            n += 1
    out[n:] = out[:2]
    return out


def _masks():
    import numpy as np
    j = np.arange(P)[:, None]
    parts = [np.tile(j == np.arange(P)[None], (1, NC))]
    for s in LEVELS:
        i = np.arange(P // 2)[None]
        parts.append(np.tile((j // (2 * s) == i // s) & (j % (2 * s) < s), (1, NC)))
    return np.concatenate(parts, axis=1).astype(np.uint32)


def kernel(**inputs):
    import numpy as np
    import concourse.bacc as bacc
    from concourse.bass_utils import run_bass_kernel_spmd

    inputs = {k: np.asarray(v) for k, v in inputs.items()}
    x_t = np.zeros((NT + 1, P, KD, TT), np.float32)
    x_t[:NT] = inputs["x"][0].reshape(NT, TT, KD, P).transpose(0, 3, 2, 1)
    par = np.zeros((P, N_PAR), np.float32)
    for at, a in ((C_MIXN, inputs["mix_norm"][0]), (C_FFNN, inputs["ffn_norm"][0]), (C_FINN, inputs["final_norm"]),
                  (C_LB, inputs["hg_lb_logits"][0]), (C_LNG, inputs["gm_ln_g"][0]), (C_HGN, inputs["hg_norm_g"][0]),
                  (C_CW, inputs["conv_w"][0]), (C_CB, inputs["conv_b"][0])):
        cols = _columns(a)
        par[:, at:at + cols.shape[1]] = cols
    arrays = {
        "x_t": x_t,
        "w_units": _units(inputs),
        "par": par,
        "masks_in": _masks(),
        "ident_in": np.eye(P, dtype=np.float32),
        "gm_wt": np.ascontiguousarray(inputs["gm_ws"][0].transpose(2, 0, 1)),
        "ln_b": np.ascontiguousarray(inputs["gm_ln_b"][0:1]),
        "gm_bs": np.ascontiguousarray(inputs["gm_bs"][0].reshape(1, NH * P)),
    }
    nc = bacc.Bacc("TRN2", target_bir_lowering=False, num_devices=1)
    args = [nc.dram_tensor(n, arrays[n].shape, mybir.dt.from_np(arrays[n].dtype), kind="ExternalInput").ap()
            for n in _ORDER]
    out = nc.dram_tensor("out", (NT + 1, P, KD, TT), F32, kind="ExternalOutput").ap()
    build(nc, *args, out)
    r = run_bass_kernel_spmd(nc, [arrays], core_ids=[0])
    got = r.results[0]["out"][1:]
    return np.ascontiguousarray(got.transpose(0, 3, 2, 1).reshape(1, SEQ, D))
```

```python
import concourse.bass as bass
from concourse import mybir

F32 = mybir.dt.float32
F32R = mybir.dt.float32r
U32 = mybir.dt.uint32
ACT = mybir.ActivationFunctionType
ALU = mybir.AluOpType

P = 128
D = 1024
SEQ = 2048
TT = 512
NT = SEQ // TT
NC = TT // P
KD = D // P
NH = 4
FF = 2816
KF = FF // P
EPS = 1e-6
TINY = 1e-30
LB_MAX = 0.999
LEVELS = [1, 2, 4, 8, 16, 32, 64]
GM_CHUNK = 64
GM_BANKS = (2, 3, 5, 7)

U_FRONT = 0
U_MIX = U_FRONT + 6 * NH
G_UNIT = [0, 4, 10, 16]
B_UNIT = [8, 14, 20, 22]
U_OUT = U_MIX + 3 * KD
U_UP = U_OUT + KD
U_DOWN = U_UP + 2 * KF
UNITS = U_DOWN + 3 * KD
DOWN_SPLIT = [0, 8, 15, KF]
B_FRONT = 1
B_MIX = B_FRONT + 3 * NH
B_OUT = B_MIX + KD
B_UP = B_OUT + KD // 2
B_DOWN = B_UP + KF
B_TILE = B_DOWN + KD // 2 - B_FRONT

C_MIXN, C_FFNN, C_FINN = 0, KD, 2 * KD
C_LB = 3 * KD
C_LNG = C_LB + NH
C_HGN = C_LNG + NH
C_CW = C_HGN + 1
C_CB = C_CW + 3 * 2 * KF
N_PAR = C_CB + 2 * KF


class Steps:

    def __init__(self, sem, names, head_start=0):
        self.sem, self.names, self.n, self.head_start = sem, names, 0, head_start

    def did(self, name):
        assert self.names[self.n % len(self.names)] == name, (self.names[self.n % len(self.names)], name)
        self.n += 1
        return self.sem, 1

    def at(self, name, turn):
        return self.sem, turn * len(self.names) + (self.names.index(name) + 1 + self.head_start)

    def before(self, turn):
        return self.sem, turn * len(self.names) + self.head_start


def halves(ap, s):
    v = ap.rearrange("p (n two s) -> p n two s", two=2, s=s)
    return v[:, :, 0, :], v[:, :, 1, :]


def blocks(ap, s):
    return ap.rearrange("p (n s) -> p n s", s=s)


def spread(ap, s):
    return ap.unsqueeze(2).broadcast_to([P, ap.shape[1], s])


def build(nc, x_t, w_units, par, masks_in, ident_in, gm_wt, ln_b, gm_bs, out):
    top = [nc.sbuf_base + (-nc.sbuf_base) % 64]

    def place(name, shape, dt=F32, at=None):
        size = 4
        for n in shape[1:]:
            size *= n
        if at is None:
            at = top[0]
            top[0] += size + (-size) % 64
            assert top[0] <= nc.sbuf_usable_end, (name, top[0])
        return nc.alloc_sbuf_tensor_at(name, shape, dt, offset=at)

    def room(size):
        at = top[0]
        top[0] += size
        return at

    BLK = TT * 4
    raw = [place(f"raw{i}", [P, KD, P]) for i in range(2)]
    w_hi = [place(f"w_hi{i}", [P, KD, P], F32R) for i in range(2)]
    w_lo = [place(f"w_lo{i}", [P, KD, P], F32R) for i in range(2)]
    h_hi = place("h_hi", [P, KD, TT], F32R)
    at_lo = room(KD * BLK)
    h_lo = place("h_lo", [P, KD, TT], F32R, at_lo)
    x_in = place("x_in", [P, KD, TT], F32, at_lo)
    res = place("res", [P, KD, TT])
    carry = place("carry", [P, NH, P])
    state = place("state", [P, NC, P])
    halo = place("halo", [P, (NT + 1) * 2 * KF, 2])
    params = place("params", [P, N_PAR])
    lower = place("lower", [P, 4, NH])
    masks = place("masks", [P, NC * P + len(LEVELS) * NC * P // 2], U32)
    ident = place("ident", [P, P])
    ones = place("ones", [P, P])
    eps = place("eps", [P, 1])
    scratch = place("scratch", [P, 8])
    gm_w = place("gm_w", [P, NH, P])
    gm_b = place("gm_b", [P, NH, P])
    stats = place("stats", [P, NC, 6])
    moments = place("moments", [P, NC, 2])
    spreads = place("spreads", [P, 2, NC])
    tok_n = place("tok_n", [P, 2, NC])
    tok_r = place("tok_r", [P, 2, NC])
    sum_r = place("sum_r", [P, TT])

    arena = room(2 * KF * BLK)
    g_hi = place("g_hi", [P, KF, TT], F32R, arena)
    g_lo = place("g_lo", [P, KF, TT], F32R, arena + KF * BLK)
    a_hi = place("a_hi", [P, NH, TT], F32R, arena)
    a_lo = place("a_lo", [P, NH, TT], F32R, arena + 4 * BLK)
    b_hi = place("b_hi", [P, NH, TT], F32R, arena + 8 * BLK)
    b_lo = place("b_lo", [P, NH, TT], F32R, arena + 12 * BLK)
    y_at = arena + 16 * BLK
    y_hi = place("y_hi", [P, KD, TT], F32R, y_at)
    y_lo = place("y_lo", [P, KD, TT], F32R, y_at + KD * BLK)
    q0 = place("q0", [P, TT], F32, y_at)
    qp = place("qp", [P, TT], F32, y_at + BLK)
    kp = {s: place(f"kp{s}", [P, TT], F32, y_at + (2 + n) * BLK)
          for n, s in enumerate(LEVELS + [P])}
    q_right = {s: place(f"qr{s}", [P, TT // 2], F32, y_at + 10 * BLK + n * BLK // 2)
               for n, s in enumerate(LEVELS)}
    t_at = y_at + 14 * BLK
    total = {}
    for s in LEVELS + [P]:
        total[s] = place(f"total{s}", [P, TT // s], F32, t_at)
        t_at += TT // s * 4
    assert t_at <= y_at + 16 * BLK
    u_act = place("u_act", [P, NH, TT], F32, y_at + 16 * BLK)
    v_tok = place("v_tok", [P, NC, NH * P], F32, y_at + 20 * BLK)
    late = y_at + 24 * BLK
    og_act = place("og_act", [P, TT], F32, late)
    i_tok = place("i_tok", [P, TT], F32, late + BLK)
    k_tok = place("k_tok", [P, TT], F32, late + 2 * BLK)
    scores = place("scores", [P, TT], F32, late + 3 * BLK)
    assert late + 4 * BLK <= arena + 2 * KF * BLK

    SLOT = BLK + 64
    pool = room(10 * SLOT)

    def temp(name, slot, width=TT):
        return place(name, [P, width], F32, pool + slot * SLOT)

    sig_f, sig_nf, sig_q, sig_og = (temp(n, i) for i, n in enumerate(("sig_f", "sig_nf", "sig_q", "sig_og")))
    i_raw, v_act, o_sq, o_rms = temp("i_raw", 4), temp("v_act", 5), temp("o_sq", 6), temp("o_rms", 7)
    o_unit, b_f32 = temp("o_unit", 8), temp("b_f32", 9)
    sum_n, diag_n = temp("sum_n", 1), temp("diag_n", 3)
    h_f32 = [temp("h_f32a", 4), temp("h_f32b", 5)]
    sq_r, diag_r = temp("sq_r", 6), temp("diag_r", 7)
    conv = [temp("conv0", 0), temp("conv1", 1)]
    silu, g_f32 = temp("silu", 2), temp("g_f32", 3)
    z = [temp("z0", 4, TT + 2), temp("z1", 5, TT + 2)]
    gate_a = [[temp("ga00", 0), temp("ga01", 1)], [place(f"ga1{j}", [P, TT], F32, late + j * BLK) for j in range(2)]]
    gate_b = [[temp("gb00", 2), temp("gb01", 3)],
              [place(f"gb1{j}", [P, TT], F32, late + (2 + j) * BLK) for j in range(2)]]
    gm_mix, a_f32 = temp("gm_mix", 8), temp("a_f32", 9)
    br_b, br_a, y_f32 = temp("br_b", 4), temp("br_a", 5), temp("y_f32", 6)
    lnb_row, bs_row = temp("lnb_row", 0), temp("bs_row", 2)

    bank = [nc.alloc_psum_tensor(f"bank{i}", [P, TT], F32) for i in range(8)]

    def sem(name):
        return nc.alloc_semaphore(name)

    par_in, consts_in, res_in, out_sent = sem("par_in"), sem("consts_in"), sem("res_in"), sem("out_sent")
    ident_here = sem("ident_here")
    x_next_in = [sem("x_next_in0"), sem("x_next_in1")]
    raw_in = [sem("raw_in0"), sem("raw_in1")]
    hi_made, lo_made, unit_done = sem("hi_made"), sem("lo_made"), sem("unit_done")
    evac = [sem("evac0"), sem("evac1")]
    N_CONST = 16 * 4

    head_act = Steps(sem("head_act"), ["sig_f", "sig_q", "sig_og", "i_tok", "k_tok", "o_sq", "v_tok", "o_rms"])
    head_pe = Steps(sem("head_pe"), ["i_tok", "s1", "diag", "k_tok", "s64_32", "s16_8", "s4_2", "update",
                                     "o", "v_tok", "o_sum"])
    names = ["forget", "floor", "qp1"]
    for s in LEVELS:
        names += [f"qr{s}", f"qp{2 * s}", f"kl{2 * s}", f"kr{2 * s}", f"t{2 * s}"]
    head_dve = Steps(sem("head_dve"), ["k"] + names + ["m1", "m0", "m64", "m32", "m16", "m8", "m4", "m2", "st0", "st1",
                                                       "st2", "st3", "st4", "inv", "unit", "b", "b_hi", "b_lo"])
    gm_dve = Steps(sem("gm_dve"), [f"bn{c}" for c in range(NC)] + [f"ag{c}" for c in range(NC)] + ["inv"]
                   + [f"vn{c}" for c in range(NC)]
                   + [f"{n}{h}" for h in range(NH) for n in ("mix", "a", "a_hi", "a_lo")])
    gm_act = Steps(sem("gm_act"), ["std"])
    gm_pe = Steps(sem("gm_pe"), [f"mix{h}" for h in range(NH)])
    mix_dve = Steps(sem("mix_dve"), [f"{n}{j}" for j in range(2) for n in ("b", "a", "y", "y_hi", "y_lo")], 1)
    res_act = Steps(sem("res_act"), ["sq"])
    res_dve = Steps(sem("res_dve"), ["sum"], 1)
    zero_dve = Steps(sem("zero_dve"), ["scores", "sum_out", "sum_down", "sum_n"])
    norm_pe = Steps(sem("norm_pe"), ["ssq", "spread"])
    norm_act = Steps(sem("norm_act"), ["rms"] + [f"hi{c}" for c in range(KD)])
    pre_act = Steps(sem("pre_act"), ["sq"])
    pre_dve = Steps(sem("pre_dve"), ["sum"], 1)
    names = ["inv", "diag"]
    for a in range(0, KD, 4):
        names.append(f"f{a}")
        for c in range(a, a + 4):
            names += ([f"f{c + 1}"] if c + 1 < a + 4 else []) + [f"lo{c}"]
    norm_dve = Steps(sem("norm_dve"), names)
    up_act = Steps(sem("up_act"), ["silu"])
    up_dve = Steps(sem("up_dve"), ["c0", "d0", "e0", "c1", "d1", "e1", "g", "g_hi", "g_lo"], 1)
    fin_pe, fin_act = Steps(sem("fin_pe"), ["ssq", "spread"]), Steps(sem("fin_act"), ["rms"])
    fin_dve = Steps(sem("fin_dve"), ["inv", "diag"] + [f"o{c}" for c in range(KD)], 1)
    pro_dve, pro_act, pro_pe, pro_pool = sem("pro_dve"), sem("pro_act"), sem("pro_pe"), sem("pro_pool")

    def par_col(c, n=1):
        return params[:, c:c + n]

    def par_dyn(c, i):
        return params[:, bass.ds(c + i, 1)]

    mask_of, at = {0: masks[:, 0:TT]}, TT
    for s in LEVELS:
        mask_of[s] = masks[:, at:at + TT // 2]
        at += TT // 2
    level_place = {1: (3, 0), 64: (5, 0), 32: (5, 1), 16: (6, 0), 8: (6, 1), 4: (7, 0), 2: (7, 1)}

    def level_out(s):
        b, half = level_place[s]
        return bank[b][:, half * TT // 2:(half + 1) * TT // 2]

    block = nc.Block()
    block.__enter__()

    @block.sync
    def _(sp):
        def load(unit, slot):
            sp.dma_start(raw[slot][:, :, :], w_units[unit]).then_inc(raw_in[slot], 16)

        def stream(t, first, last):
            with sp.Fori(0, (last - first) // 2) as i:
                for j in range(2):
                    sp.wait_ge(lo_made, t * UNITS + i * 2 + (first + j + 1))
                    load(i * 2 + (first + j + 2), j)

        def load_x(tile):
            for j in range(2):
                part = slice(j * KD // 2, (j + 1) * KD // 2)
                sp.dma_start(x_in[:, part, :], x_t[tile, :, part, :]).then_inc(x_next_in[j], 16)

        load_x(0)
        sp.dma_start(params[:, :], par).then_inc(par_in, 16)
        sp.dma_start(ident[:, :], ident_in).then_inc(ident_here, 16)
        load(0, 0)
        load(1, 1)
        for a, b in ((gm_w[:, :, :], gm_wt), (lnb_row[:, :], ln_b.broadcast_to([P, NH * P])),
                     (bs_row[:, :], gm_bs.broadcast_to([P, NH * P])), (masks[:, :], masks_in)):
            sp.dma_start(a, b).then_inc(consts_in, 16)
        with sp.Fori(0, NT) as t:
            stream(t, 0, 36)
            sp.wait_ge(*fin_dve.before(t + 1))
            sp.dma_start(out[t], res[:, :, :]).then_inc(out_sent, 16)
            stream(t, 36, 44)
            sp.wait_ge(out_sent, t * 16 + 16)
            sp.dma_start(res[:, :, :], x_t[t]).then_inc(res_in, 16)
            stream(t, 44, U_DOWN + 4)
            sp.wait_ge(unit_done, t * UNITS + U_DOWN)
            load_x(t + 1)
            stream(t, U_DOWN + 4, UNITS)
        for c in range(0, KD, 2):
            sp.wait_ge(*fin_dve.at(f"o{c + 1}", NT))
            sp.dma_start(out[NT, :, c:c + 2, :], res[:, c:c + 2, :]).then_inc(out_sent, 16)
        sp.wait_ge(out_sent, 16 * (NT + KD // 2))

    @block.gpsimd
    def _(po):
        po.memset(carry[:, :, :], 0.0).then_inc(pro_pool, 1)
        po.memset(halo[:, 0:2 * KF, :], 0.0).then_inc(pro_pool, 1)
        po.memset(res[:, :, :], 0.0).then_inc(pro_pool, 1)
        po.memset(sum_r[:, :], 0.0).then_inc(pro_pool, 1)
        with po.Fori(0, (NT * UNITS + 2) // 2) as i:
            for j in range(2):
                po.wait_ge(hi_made, i * 2 + (j + 1))
                po.tensor_tensor(w_lo[j][:, :, :], raw[j][:, :, :], w_hi[j][:, :, :].bitcast(F32),
                                 ALU.subtract).then_inc(lo_made, 1)

    @block.scalar
    def _(act):
        def weights_hi(t, u, i=0):
            slot = u % 2
            act.wait_ge(unit_done, t * UNITS + i + (u + 1))
            act.wait_ge(raw_in[slot], t * (8 * UNITS) + i * 8 + 16 * (u // 2 + 2))
            act.activation(w_hi[slot][:, :, :], raw[slot][:, :, :], ACT.Copy).then_inc(hi_made, 1)

        def pre_square(turn, c):
            if c % (KD // 2) == 0:
                act.wait_ge(x_next_in[c // (KD // 2)], turn * 16 + 16)
            if c >= 2:
                act.wait_ge(*pre_dve.before(turn * KD + c - 1))
            act.activation(h_f32[c % 2][:, :], x_in[:, c, :], ACT.Square).then_inc(*pre_act.did("sq"))

        def norm_rms(turn):
            act.wait_ge(*norm_pe.at("ssq", turn))
            act.activation(tok_n[:, 0, :], bank[2][:, 0:NC], ACT.Sqrt, bias=eps[:, 0:1],
                           scale=1.0 / D).then_inc(*norm_act.did("rms"))

        def norm_hi(turn, a, b):
            for c in range(a, b):
                act.wait_ge(*norm_dve.at(f"f{c}", turn))
                act.activation(h_hi[:, c, :], h_f32[c % 2][:, :], ACT.Copy).then_inc(*norm_act.did(f"hi{c}"))

        for c in range(KD):
            pre_square(0, c)
        for j in range(2):
            act.sem_inc(evac[j], 1)
            act.wait_ge(raw_in[j], 16)
            act.activation(w_hi[j][:, :, :], raw[j][:, :, :], ACT.Copy).then_inc(hi_made, 1)
        act.wait_ge(pro_dve, 1)
        norm_rms(0)
        norm_hi(0, 0, KD)
        act.wait_ge(pro_dve, 2)
        act.activation(lower[:, 1, :], lower[:, 0, :], ACT.Exp).then_inc(pro_act, 1)
        act.wait_ge(pro_pool, 4)
        act.wait_ge(pro_dve, 9)

        with act.Fori(0, NT) as t:
            with act.Fori(0, NH) as h:
                it = t * NH + h
                u = h * 6
                weights_hi(t, 0, u)
                act.activation(sig_f[:, :], bank[0][:, :], ACT.Sigmoid).then_inc(*head_act.did("sig_f"))
                act.activation(sig_nf[:, :], bank[0][:, :], ACT.Sigmoid, scale=-1.0).then_inc(evac[0], 1)
                weights_hi(t, 1, u)
                act.activation(sig_q[:, :], bank[1][:, :], ACT.Sigmoid).then_inc(*head_act.did("sig_q"))
                weights_hi(t, 2, u)
                act.activation(i_raw[:, :], bank[0][:, :], ACT.Copy).then_inc(evac[0], 1)
                weights_hi(t, 3, u)
                act.activation(sig_og[:, :], bank[1][:, :], ACT.Sigmoid).then_inc(*head_act.did("sig_og"))
                act.wait_ge(*head_pe.at("i_tok", it))
                act.activation(i_tok[:, :], bank[2][:, :], ACT.Copy).then_inc(*head_act.did("i_tok"))
                weights_hi(t, 4, u)
                act.activation(v_act[:, :], bank[0][:, :], ACT.Gelu).then_inc(evac[0], 1)
                act.wait_ge(*head_pe.at("k_tok", it))
                act.activation(k_tok[:, :], bank[2][:, :], ACT.Copy).then_inc(*head_act.did("k_tok"))
                weights_hi(t, 5, u)
                act.activation(u_act[:, h, :], bank[1][:, :], ACT.Gelu).then_inc(evac[1], 1)
                act.wait_ge(*head_pe.at("o", it))
                act.activation(o_sq[:, :], bank[4][:, :], ACT.Square).then_inc(*head_act.did("o_sq"))
                act.wait_ge(*head_pe.at("v_tok", it))
                act.activation(v_tok[:, :, bass.ts(h, P)], blocks(bank[3][:, :], P),
                               ACT.Copy).then_inc(*head_act.did("v_tok"))
                act.wait_ge(*head_pe.at("o_sum", it))
                act.activation(o_rms[:, :], bank[5][:, :], ACT.Sqrt, bias=eps[:, 0:1],
                               scale=1.0 / P).then_inc(*head_act.did("o_rms"))

            act.wait_ge(*gm_dve.at(f"ag{NC - 1}", t))
            act.activation(spreads[:, 0, :], moments[:, :, 1], ACT.Sqrt, bias=eps[:, 0:1]).then_inc(*gm_act.did("std"))

            def gates(p):
                if p >= 2:
                    act.wait_ge(*mix_dve.before(t * (KD // 2) + (p - 1)))
                for j in range(2):
                    weights_hi(t, U_MIX + G_UNIT[p] + 2 * j)
                    act.activation(gate_a[p % 2][j][:, :], bank[0][:, :], ACT.Sigmoid).then_inc(evac[0], 1)
                    weights_hi(t, U_MIX + G_UNIT[p] + 2 * j + 1)
                    act.activation(gate_b[p % 2][j][:, :], bank[1][:, :], ACT.Sigmoid).then_inc(evac[1], 1)

            def branches(p):
                for j in range(2):
                    weights_hi(t, U_MIX + B_UNIT[p] + j)

            def final_rms(turn):
                act.wait_ge(*fin_pe.at("ssq", turn))
                act.activation(tok_r[:, 0, :], bank[6][:, 0:NC], ACT.Sqrt, bias=eps[:, 0:1],
                               scale=1.0 / D).then_inc(*fin_act.did("rms"))

            final_rms(t)
            gates(0)
            for p in range(1, KD // 2):
                gates(p)
                branches(p - 1)
            branches(KD // 2 - 1)

            with act.Fori(0, KD // 2) as p:
                for j in range(2):
                    weights_hi(t, U_OUT + j, p * 2)
                    act.wait_ge(evac[j], t * B_TILE + p + (B_OUT + 1))
                    act.wait_ge(*res_dve.before(t * (2 * KD) + p * 2 + j))
                    act.activation(sq_r[:, :], res[:, p * 2 + j, :],
                                   ACT.Square).then_inc(*res_act.did("sq"))
            norm_rms(t * 2 + 1)
            norm_hi(t * 2 + 1, 0, KD)

            with act.Fori(0, KF) as f:
                it = t * KF + f
                act.wait_ge(*up_dve.before(it))
                for j in range(2):
                    weights_hi(t, U_UP + j, f * 2)
                    col = t * (2 * KF) + f + j * KF
                    act.activation(z[j][:, 0:2], halo[:, col, :], ACT.Copy)
                    act.activation(halo[:, col + 2 * KF, :], bank[j][:, TT - 2:TT], ACT.Copy)
                    act.activation(z[j][:, 2:TT + 2], bank[j][:, :], ACT.Copy).then_inc(evac[j], 1)
                act.wait_ge(*up_dve.at("e0", it))
                act.activation(silu[:, :], conv[0][:, :], ACT.Silu).then_inc(*up_act.did("silu"))

            for p in range(KD // 2):
                for j in range(2):
                    for part in range(3):
                        weights_hi(t, U_DOWN + 6 * p + 3 * j + part)
                        if p == 1 and part < 2:
                            for c in range(4 * j + 2 * part, 4 * j + 2 * part + 2):
                                pre_square(t + 1, c)
                        if p == 2 and j == 0 and part == 0:
                            norm_rms(t * 2 + 2)
                        if (p, j) in ((2, 1), (3, 0)) and part < 2:
                            norm_hi(t * 2 + 2, 4 * (p - 2) + 2 * part, 4 * (p - 2) + 2 * part + 2)
                    c = 2 * p + j
                    act.wait_ge(evac[j], t * B_TILE + (B_DOWN + p + 1))
                    act.wait_ge(*res_dve.before(t * (2 * KD) + KD + c))
                    act.activation(sq_r[:, :], res[:, c, :], ACT.Square).then_inc(*res_act.did("sq"))
        final_rms(NT)

    @block.vector
    def _(dve):
        def inverse(tok, diag, steps, turn):
            dve.reciprocal(tok[:, 1, :], tok[:, 0, :]).then_inc(*steps.did("inv"))
            dve.wait_ge(*steps.at("inv", turn))
            dve.tensor_tensor(blocks(diag[:, :], P), ident[:, :].unsqueeze(1).broadcast_to([P, NC, P]),
                              spread(tok[:, 1, :], P), ALU.mult).then_inc(*steps.did("diag"))

        def pre_sum(turn, c):
            dve.wait_ge(*pre_act.at("sq", turn * KD + c))
            dve.wait_ge(*pre_dve.before(turn * KD + c))
            dve.tensor_tensor(sum_n[:, :], sum_n[:, :], h_f32[c % 2][:, :], ALU.add).then_inc(*pre_dve.did("sum"))

        def norm_inv(turn):
            dve.wait_ge(*norm_act.at("rms", turn))
            inverse(tok_n, diag_n, norm_dve, turn)

        def norm_parts(turn, src, col, a, b):
            def whole(c):
                if c == 0:
                    dve.wait_ge(*norm_pe.at("spread", turn))
                else:
                    dve.wait_ge(*norm_dve.at(f"lo{c - 2}" if c > 1 else "diag", turn))
                dve.scalar_tensor_tensor(out=h_f32[c % 2][:, :], in0=src[:, c, :], scalar=par_col(col + c),
                                         in1=bank[3][:, :], op0=ALU.mult, op1=ALU.mult).then_inc(*norm_dve.did(f"f{c}"))
            whole(a)
            for c in range(a, b):
                if c + 1 < b:
                    whole(c + 1)
                dve.wait_ge(*norm_act.at(f"hi{c}", turn))
                dve.tensor_tensor(h_lo[:, c, :], h_f32[c % 2][:, :], h_hi[:, c, :].bitcast(F32),
                                  ALU.subtract).then_inc(*norm_dve.did(f"lo{c}"))

        for steps in (mix_dve, res_dve, pre_dve, up_dve, fin_dve):
            dve.sem_inc(steps.sem, steps.head_start)
        dve.memset(sum_n[:, :], 0.0)
        dve.memset(ones[:, :], 1.0)
        dve.memset(eps[:, :], EPS).then_inc(pro_dve, 1)
        dve.wait_ge(pro_dve, 1)
        for c in range(KD):
            pre_sum(0, c)
        dve.wait_ge(ident_here, 16)
        dve.wait_ge(par_in, 16)
        norm_inv(0)
        norm_parts(0, x_in, C_MIXN, 0, KD // 2)
        norm_parts(0, x_in, C_MIXN, KD // 2, KD)
        lb = par_col(C_LB, NH)
        dve.tensor_tensor(lower[:, 0, :], lb, lb, ALU.subtract).then_inc(pro_dve, 1)
        dve.wait_ge(pro_act, 1)
        dve.reciprocal(lower[:, 2, :], lower[:, 1, :]).then_inc(pro_dve, 1)
        dve.wait_ge(pro_dve, 3)
        dve.tensor_tensor(lower[:, 3, :], lower[:, 1, :], lower[:, 2, :], ALU.mult).then_inc(pro_dve, 1)
        dve.wait_ge(pro_dve, 4)
        dve.tensor_tensor(lower[:, 1, :], lower[:, 3, :], lower[:, 3, :], ALU.subtract).then_inc(pro_dve, 1)
        dve.wait_ge(pro_dve, 5)
        dve.tensor_scalar(lower[:, 2, :], lower[:, 1, :], 0.0, LB_MAX, ALU.max, ALU.min).then_inc(pro_dve, 1)
        dve.wait_ge(pro_dve, 6)
        dve.tensor_scalar(lower[:, 3, :], lower[:, 2, :], -1.0, 1.0, ALU.mult, ALU.add).then_inc(pro_dve, 1)
        dve.wait_ge(consts_in, N_CONST)
        dve.memset(gm_w[GM_CHUNK:P, :, 0:GM_CHUNK], 0.0).then_inc(pro_dve, 1)
        dve.wait_ge(pro_pe, 1)
        dve.tensor_tensor(gm_b[:, :, :], blocks(bank[4][:, :], P), blocks(bs_row[:, :], P), ALU.add).then_inc(pro_dve, 1)
        dve.wait_ge(pro_pool, 4)
        dve.wait_ge(pro_dve, 9)

        with dve.Fori(0, NT) as t:
            dve.memset(scores[:, :], 0.0).then_inc(*zero_dve.did("scores"))
            with dve.Fori(0, NH) as h:
                it = t * NH + h
                used = t * B_TILE + h * 3 + B_FRONT
                keep = lower[:, 3, bass.ds(h, 1)]

                def then(name):
                    dve.wait_ge(*head_dve.at(name, it))

                dve.wait_ge(evac[0], used + 1)
                dve.tensor_scalar(kp[1][:, :], sig_nf[:, :], keep, None, ALU.mult).then_inc(*head_dve.did("k"))
                dve.wait_ge(*head_act.at("sig_f", it))
                dve.tensor_scalar(total[1][:, :], sig_f[:, :], keep, lower[:, 2, bass.ds(h, 1)], ALU.mult,
                                  ALU.add).then_inc(*head_dve.did("forget"))
                then("forget")
                dve.tensor_scalar(total[1][:, :], total[1][:, :], TINY, None, ALU.max).then_inc(*head_dve.did("floor"))
                dve.wait_ge(*head_act.at("sig_q", it))
                dve.tensor_tensor(q0[:, :], sig_q[:, :], bank[1][:, :], ALU.mult).then_inc(evac[1], 1)
                then("floor")
                dve.wait_ge(evac[1], used + 1)
                dve.tensor_tensor(qp[:, :], q0[:, :], total[1][:, :], ALU.mult).then_inc(*head_dve.did("qp1"))
                for s in LEVELS:
                    then(f"t{s}" if s > 1 else "qp1")
                    q_l, q_r = halves(qp[:, :], s)
                    k_l, k_r = halves(kp[s][:, :], s)
                    k2_l, k2_r = halves(kp[2 * s][:, :], s)
                    t_l, t_r = halves(total[s][:, :], 1)
                    t_l, t_r = t_l[:, :, 0], t_r[:, :, 0]
                    dve.tensor_copy(blocks(q_right[s][:, :], s), q_r).then_inc(*head_dve.did(f"qr{s}"))
                    then(f"qr{s}")
                    dve.tensor_tensor(q_r, blocks(q_right[s][:, :], s), spread(t_l, s),
                                      ALU.mult).then_inc(*head_dve.did(f"qp{2 * s}"))
                    dve.tensor_tensor(k2_l, k_l, spread(t_r, s), ALU.mult).then_inc(*head_dve.did(f"kl{2 * s}"))
                    dve.tensor_copy(k2_r, k_r).then_inc(*head_dve.did(f"kr{2 * s}"))
                    dve.tensor_tensor(total[2 * s][:, :], t_l, t_r, ALU.mult).then_inc(*head_dve.did(f"t{2 * s}"))
                dve.wait_ge(*head_act.at("sig_og", it))
                dve.tensor_tensor(og_act[:, :], sig_og[:, :], bank[1][:, :], ALU.mult).then_inc(evac[1], 1)

                for n, (s, made, before) in enumerate(((1, "s1", f"t{P}"), (0, "diag", "m1"), (64, "s64_32", "m0"),
                                                       (32, "s64_32", "m64"), (16, "s16_8", "m32"),
                                                       (8, "s16_8", "m16"), (4, "s4_2", "m8"), (2, "s4_2", "m4"))):
                    dve.wait_ge(*zero_dve.at("scores", t))
                    dve.wait_ge(*head_pe.at(made, it))
                    then(before)
                    dve.memset(scratch[:, n:n + 1], 0.0)
                    if s:
                        dve.copy_predicated(halves(scores[:, :], s)[1], blocks(mask_of[s], s),
                                            blocks(level_out(s), s)).then_inc(*head_dve.did(f"m{s}"))
                    else:
                        dve.copy_predicated(scores[:, :], mask_of[0], bank[4][:, :]).then_inc(*head_dve.did("m0"))
                dve.tensor_copy(state[:, 0, :], carry[:, h, :]).then_inc(*head_dve.did("st0"))
                dve.wait_ge(*head_pe.at("update", it))
                for c in range(NC):
                    then(f"st{c}")
                    dve.scalar_tensor_tensor(out=state[:, c + 1, :] if c + 1 < NC else carry[:, h, :],
                                             in0=state[:, c, :], scalar=total[P][:, c:c + 1],
                                             in1=bank[2][:, c * P:(c + 1) * P], op0=ALU.mult,
                                             op1=ALU.add).then_inc(*head_dve.did(f"st{c + 1}"))
                dve.wait_ge(*head_act.at("o_rms", it))
                dve.reciprocal(o_rms[:, :], o_rms[:, :]).then_inc(*head_dve.did("inv"))
                then("inv")
                dve.tensor_tensor(o_unit[:, :], o_rms[:, :], bank[4][:, :], ALU.mult).then_inc(*head_dve.did("unit"))
                then("unit")
                dve.scalar_tensor_tensor(out=b_f32[:, :], in0=o_unit[:, :], scalar=par_col(C_HGN), in1=og_act[:, :],
                                         op0=ALU.mult, op1=ALU.mult).then_inc(*head_dve.did("b"))
                then("b")
                dve.tensor_scalar(b_hi[:, h, :], b_f32[:, :], 1.0, None, ALU.mult).then_inc(*head_dve.did("b_hi"))
                then("b_hi")
                dve.tensor_tensor(b_lo[:, h, :], b_f32[:, :], b_hi[:, h, :].bitcast(F32),
                                  ALU.subtract).then_inc(*head_dve.did("b_lo"))

            dve.wait_ge(*head_act.at("v_tok", t * NH + (NH - 1)))
            for c in range(NC):
                dve.bn_stats(out=stats[:, c, :], in_=v_tok[:, c, :]).then_inc(*gm_dve.did(f"bn{c}"))
            dve.wait_ge(*gm_dve.at(f"bn{NC - 1}", t))
            dve.memset(scratch[:, 0:1], 0.0)
            for c in range(NC):
                dve.bn_aggr(out=moments[:, c, :], in_=stats[:, c, :]).then_inc(*gm_dve.did(f"ag{c}"))
            dve.wait_ge(*fin_act.at("rms", t))
            inverse(tok_r, diag_r, fin_dve, t)
            dve.wait_ge(*gm_act.at("std", t))
            dve.reciprocal(spreads[:, 1, :], spreads[:, 0, :]).then_inc(*gm_dve.did("inv"))
            dve.wait_ge(*gm_dve.at("inv", t))
            for c in range(NC):
                dve.tensor_scalar(v_tok[:, c, :], v_tok[:, c, :], moments[:, c, 0:1], spreads[:, 1, c:c + 1],
                                  ALU.subtract, ALU.mult).then_inc(*gm_dve.did(f"vn{c}"))
            for h in range(NH):
                dve.wait_ge(*gm_pe.at(f"mix{h}", t))
                dve.scalar_tensor_tensor(out=blocks(gm_mix[:, :], P), in0=blocks(bank[GM_BANKS[h]][:, :], P),
                                         scalar=par_col(C_LNG + h),
                                         in1=gm_b[:, h, :].unsqueeze(1).broadcast_to([P, NC, P]),
                                         op0=ALU.mult, op1=ALU.add).then_inc(*gm_dve.did(f"mix{h}"))
                dve.wait_ge(*gm_dve.at(f"mix{h}", t))
                dve.tensor_tensor(a_f32[:, :], gm_mix[:, :], u_act[:, h, :], ALU.mult).then_inc(*gm_dve.did(f"a{h}"))
                dve.wait_ge(*gm_dve.at(f"a{h}", t))
                dve.tensor_copy(a_hi[:, h, :], a_f32[:, :]).then_inc(*gm_dve.did(f"a_hi{h}"))
                dve.wait_ge(*gm_dve.at(f"a_hi{h}", t))
                dve.tensor_tensor(a_lo[:, h, :], a_f32[:, :], a_hi[:, h, :].bitcast(F32),
                                  ALU.subtract).then_inc(*gm_dve.did(f"a_lo{h}"))

            def final_out(turn):
                dve.wait_ge(*fin_pe.at("spread", turn))
                for c in range(KD):
                    dve.scalar_tensor_tensor(out=res[:, c, :], in0=res[:, c, :], scalar=par_col(C_FINN + c),
                                             in1=bank[4][:, :], op0=ALU.mult,
                                             op1=ALU.mult).then_inc(*fin_dve.did(f"o{c}"))

            final_out(t)

            for p in range(KD // 2):
                def then(name):
                    dve.wait_ge(*mix_dve.at(name, t * (KD // 2) + p))

                for j in range(2):
                    dve.wait_ge(unit_done, t * UNITS + (U_MIX + B_UNIT[p] + j + 1))
                    dve.wait_ge(evac[1], t * B_TILE + (B_MIX + 2 * p + j + 1))
                    dve.tensor_tensor(br_b[:, :], gate_b[p % 2][j][:, :], bank[4 + j][:, :],
                                      ALU.mult).then_inc(*mix_dve.did(f"b{j}"))
                    dve.tensor_tensor(br_a[:, :], gate_a[p % 2][j][:, :], bank[6 + j][:, :],
                                      ALU.mult).then_inc(*mix_dve.did(f"a{j}"))
                    then(f"a{j}")
                    dve.tensor_tensor(y_f32[:, :], br_a[:, :], br_b[:, :], ALU.add).then_inc(*mix_dve.did(f"y{j}"))
                    then(f"y{j}")
                    c = 2 * p + j
                    dve.tensor_copy(y_hi[:, c, :], y_f32[:, :]).then_inc(*mix_dve.did(f"y_hi{j}"))
                    then(f"y_hi{j}")
                    dve.tensor_tensor(y_lo[:, c, :], y_f32[:, :], y_hi[:, c, :].bitcast(F32),
                                      ALU.subtract).then_inc(*mix_dve.did(f"y_lo{j}"))

            dve.memset(sum_r[:, :], 0.0).then_inc(*zero_dve.did("sum_out"))
            with dve.Fori(0, KD // 2) as p:
                dve.wait_ge(*zero_dve.at("sum_out", t))
                dve.wait_ge(res_in, t * 16 + 16)
                for j in range(2):
                    dve.wait_ge(unit_done, t * UNITS + p * 2 + (U_OUT + j + 1))
                    res_c = res[:, p * 2 + j, :]
                    dve.tensor_tensor(res_c, res_c, bank[j][:, :], ALU.add).then_inc(evac[j], 1)
                    dve.wait_ge(*res_act.at("sq", t * (2 * KD) + p * 2 + j))
                    dve.tensor_tensor(sum_r[:, :], sum_r[:, :], sq_r[:, :], ALU.add).then_inc(*res_dve.did("sum"))
            norm_inv(t * 2 + 1)
            norm_parts(t * 2 + 1, res, C_FFNN, 0, KD // 2)
            norm_parts(t * 2 + 1, res, C_FFNN, KD // 2, KD)

            with dve.Fori(0, KF) as f:
                it = t * KF + f

                def then(name):
                    dve.wait_ge(*up_dve.at(name, it))

                for j in range(2):
                    ch = f + j * KF
                    dve.wait_ge(evac[j], t * B_TILE + f + (B_UP + 1))
                    dve.tensor_scalar(conv[j][:, :], z[j][:, 2:TT + 2], par_dyn(C_CW + 4 * KF, ch), par_dyn(C_CB, ch),
                                      ALU.mult, ALU.add).then_inc(*up_dve.did(f"c{j}"))
                    for tap, name, before in ((1, "d", "c"), (0, "e", "d")):
                        then(f"{before}{j}")
                        dve.scalar_tensor_tensor(out=conv[j][:, :], in0=z[j][:, tap:TT + tap],
                                                 scalar=par_dyn(C_CW + 2 * KF * tap, ch), in1=conv[j][:, :],
                                                 op0=ALU.mult, op1=ALU.add).then_inc(*up_dve.did(f"{name}{j}"))
                dve.wait_ge(*up_act.at("silu", it))
                then("e1")
                dve.tensor_tensor(g_f32[:, :], silu[:, :], conv[1][:, :], ALU.mult).then_inc(*up_dve.did("g"))
                then("g")
                dve.tensor_scalar(g_hi[:, f, :], g_f32[:, :], 1.0, None, ALU.mult).then_inc(*up_dve.did("g_hi"))
                then("g_hi")
                dve.tensor_tensor(g_lo[:, f, :], g_f32[:, :], g_hi[:, f, :].bitcast(F32),
                                  ALU.subtract).then_inc(*up_dve.did("g_lo"))

            dve.memset(sum_r[:, :], 0.0).then_inc(*zero_dve.did("sum_down"))
            dve.memset(sum_n[:, :], 0.0).then_inc(*zero_dve.did("sum_n"))
            dve.wait_ge(*zero_dve.at("sum_n", t))
            for p in range(KD // 2):
                if p == 2:
                    norm_inv(t * 2 + 2)
                for j in range(2):
                    if (p, j) in ((2, 1), (3, 0)):
                        norm_parts(t * 2 + 2, x_in, C_MIXN, 4 * (p - 2), 4 * (p - 1))
                    if p == 1:
                        for c in range(4 * j, 4 * j + 4):
                            pre_sum(t + 1, c)
                    c = 2 * p + j
                    dve.wait_ge(unit_done, t * UNITS + (U_DOWN + 3 * c + 3))
                    dve.tensor_tensor(res[:, c, :], res[:, c, :], bank[j][:, :], ALU.add).then_inc(evac[j], 1)
                    dve.wait_ge(*res_act.at("sq", t * (2 * KD) + KD + c))
                    dve.tensor_tensor(sum_r[:, :], sum_r[:, :], sq_r[:, :], ALU.add).then_inc(*res_dve.did("sum"))
        dve.wait_ge(*fin_act.at("rms", NT))
        inverse(tok_r, diag_r, fin_dve, NT)
        final_out(NT)

    @block.tensor
    def _(pe):
        def products(t, u, i, dst, rhs_hi, rhs_lo, n, first=True, last=True, off=0, ready=None, done=True):
            slot = u % 2
            if ready is None:
                pe.wait_ge(hi_made, t * UNITS + i + (u + 1))
                for k in range(n):
                    pe.matmul(dst, w_hi[slot][:, off + k, :], rhs_hi(k), start=first and k == 0, stop=False)
                    pe.matmul(dst, w_hi[slot][:, off + k, :], rhs_lo(k), start=False, stop=False)
                pe.wait_ge(lo_made, t * UNITS + i + (u + 1))
                for k in range(n):
                    mm = pe.matmul(dst, w_lo[slot][:, off + k, :], rhs_hi(k), start=False, stop=last and k == n - 1)
            else:
                pe.wait_ge(lo_made, t * UNITS + i + (u + 1))
                for k in range(n):
                    pe.wait_ge(*ready[0](k))
                    pe.matmul(dst, w_hi[slot][:, off + k, :], rhs_hi(k), start=first and k == 0, stop=False)
                    pe.matmul(dst, w_lo[slot][:, off + k, :], rhs_hi(k), start=False, stop=False)
                    pe.wait_ge(*ready[1](k))
                    mm = pe.matmul(dst, w_hi[slot][:, off + k, :], rhs_lo(k), start=False, stop=last and k == n - 1)
            if done:
                mm.then_inc(unit_done, 1)

        def from_h(t, u, i, b, uses, ready=None):
            pe.wait_ge(evac[b], uses)
            products(t, u, i, bank[b][:, :], lambda k: h_hi[:, k, :], lambda k: h_lo[:, k, :], KD, ready=ready)

        def token_sums(dst, sums):
            for c in range(NC):
                mm = pe.matmul(dst[:, c:c + 1], sums[:, c * P:(c + 1) * P], ones[:, 0:1], start=True, stop=True)
            return mm

        def norm_spread(turn):
            pe.wait_ge(*norm_dve.at("diag", turn))
            pe.matmul(bank[3][:, :], ones[:, :], diag_n[:, :], start=True, stop=True).then_inc(*norm_pe.did("spread"))

        def final_spread(turn):
            pe.wait_ge(*fin_dve.at("diag", turn))
            pe.matmul(bank[4][:, :], ones[:, :], diag_r[:, :], start=True, stop=True).then_inc(*fin_pe.did("spread"))

        def flip(dst, src):
            for c in range(NC):
                mm = pe.transpose(dst[:, c * P:(c + 1) * P], src[:, c * P:(c + 1) * P], ident[:, :])
            return mm

        def level(s):
            dst = level_out(s)
            for c in range(NC):
                mm = pe.matmul(dst[:, c * P // 2:(c + 1) * P // 2], kp[s][:, c * P:(c + 1) * P],
                               q_right[s][:, c * P // 2:(c + 1) * P // 2], start=True, stop=True)
            return mm

        pe.wait_ge(*pre_dve.at("sum", KD - 1))
        token_sums(bank[2], sum_n).then_inc(*norm_pe.did("ssq"))
        norm_spread(0)
        pe.wait_ge(consts_in, N_CONST)
        pe.wait_ge(pro_dve, 8)
        for h in range(NH):
            mm = pe.matmul(bank[4][:, h * P:(h + 1) * P], lnb_row[:, h * P:(h + 1) * P], gm_w[:, h, :],
                           start=True, stop=True)
        mm.then_inc(pro_pe, 1)

        with pe.Fori(0, NT) as t:
            with pe.Fori(0, NH) as h:
                it = t * NH + h
                u = h * 6
                used = t * B_TILE + h * 3 + B_FRONT
                from_h(t, 0, u, 0, used, (lambda k: norm_act.at(f"hi{k}", t * 2),
                                          lambda k: norm_dve.at(f"lo{k}", t * 2)))
                from_h(t, 1, u, 1, used)
                from_h(t, 2, u, 0, used + 1)
                from_h(t, 3, u, 1, used + 1)
                pe.wait_ge(evac[0], used + 2)
                flip(bank[2], i_raw).then_inc(*head_pe.did("i_tok"))
                pe.wait_ge(*head_dve.at("qr1", it))
                level(1).then_inc(*head_pe.did("s1"))
                for c in range(NC):
                    cols = slice(c * P, (c + 1) * P)
                    mm = pe.matmul(bank[4][:, cols], kp[1][:, cols], q0[:, cols], start=True, stop=True)
                mm.then_inc(*head_pe.did("diag"))
                from_h(t, 4, u, 0, used + 2)
                pe.wait_ge(*head_act.at("i_tok", it))
                pe.wait_ge(*head_dve.at(f"t{P}", it))
                flip(bank[2], kp[P]).then_inc(*head_pe.did("k_tok"))
                for a, b in ((64, 32), (16, 8), (4, 2)):
                    level(a)
                    level(b).then_inc(*head_pe.did(f"s{a}_{b}"))
                from_h(t, 5, u, 1, used + 2)
                pe.wait_ge(evac[0], used + 3)
                pe.wait_ge(*head_dve.at("m2", it))
                pe.wait_ge(*head_act.at("k_tok", it))
                for c in range(NC):
                    cols = slice(c * P, (c + 1) * P)
                    mm = pe.matmul(bank[2][:, cols], k_tok[:, cols], i_tok[:, cols], start=True, stop=True)
                mm.then_inc(*head_pe.did("update"))
                for c in range(NC):
                    cols = slice(c * P, (c + 1) * P)
                    pe.matmul(bank[4][:, cols], i_tok[:, cols], scores[:, cols], start=True, stop=False)
                    pe.wait_ge(*head_dve.at(f"st{c}", it))
                    mm = pe.matmul(bank[4][:, cols], state[:, c, :], qp[:, cols], start=False, stop=True)
                mm.then_inc(*head_pe.did("o"))
                flip(bank[3], v_act).then_inc(*head_pe.did("v_tok"))
                pe.wait_ge(*head_act.at("o_sq", it))
                pe.wait_ge(*head_dve.at("st4", it))
                pe.matmul(bank[5][:, :], ones[:, :], o_sq[:, :], start=True,
                          stop=True).then_inc(*head_pe.did("o_sum"))

            def gates(u, uses):
                for j in range(2):
                    from_h(t, U_MIX + 2 * j, u, 0, uses + j)
                    from_h(t, U_MIX + 2 * j + 1, u, 1, uses + j)

            def branches(u, it, a_ready=None):
                pe.wait_ge(*mix_dve.before(it))
                for j in range(2):
                    products(t, U_MIX + j, u, bank[4 + j][:, :], lambda k: b_hi[:, k, :],
                             lambda k: b_lo[:, k, :], NH, done=False)
                    products(t, U_MIX + j, u, bank[6 + j][:, :], lambda k: a_hi[:, k, :],
                             lambda k: a_lo[:, k, :], NH, off=NH, ready=a_ready if j == 0 else None)

            pe.wait_ge(*res_dve.before(t * (2 * KD)))
            token_sums(bank[6], sum_r).then_inc(*fin_pe.did("ssq"))
            gates(G_UNIT[0], t * B_TILE + B_MIX)
            final_spread(t)
            pe.wait_ge(*gm_dve.at(f"vn{NC - 1}", t))
            for h in range(NH):
                for c in range(NC):
                    mm = pe.matmul(bank[GM_BANKS[h]][:, c * P:(c + 1) * P], v_tok[:, c, h * P:(h + 1) * P],
                                   gm_w[:, h, :], start=True, stop=True)
                mm.then_inc(*gm_pe.did(f"mix{h}"))
            gates(G_UNIT[1], t * B_TILE + (B_MIX + 2))
            pe.wait_ge(*head_dve.at("b_lo", t * NH + (NH - 1)))
            pe.wait_ge(*fin_dve.before(t + 1))
            branches(B_UNIT[0], t * (KD // 2), (lambda k: gm_dve.at(f"a_lo{k}", t),) * 2)
            with pe.Fori(0, KD // 2 - 2) as p:
                gates(p * (G_UNIT[3] - G_UNIT[2]) + G_UNIT[2], t * B_TILE + p * 2 + (B_MIX + 4))
                branches(p * (G_UNIT[3] - G_UNIT[2]) + B_UNIT[1], t * (KD // 2) + p + 1)
            branches(B_UNIT[3], t * (KD // 2) + (KD // 2 - 1))

            def project(i, uses, ready=None):
                for j in range(2):
                    pe.wait_ge(evac[j], uses)
                    products(t, U_OUT + j, i, bank[j][:, :], lambda k: y_hi[:, k, :], lambda k: y_lo[:, k, :], KD,
                             ready=ready if j == 0 else None)

            project(0, t * B_TILE + B_OUT, (lambda k: mix_dve.at(f"y_hi{k % 2}", t * (KD // 2) + k // 2),
                                            lambda k: mix_dve.at(f"y_lo{k % 2}", t * (KD // 2) + k // 2)))
            with pe.Fori(1, KD // 2) as p:
                project(p * 2, t * B_TILE + p + B_OUT)
            pe.wait_ge(*res_dve.before(t * (2 * KD) + KD))
            token_sums(bank[2], sum_r).then_inc(*norm_pe.did("ssq"))
            norm_spread(t * 2 + 1)

            for j in range(2):
                pe.wait_ge(evac[j], t * B_TILE + B_UP)
                pe.wait_ge(lo_made, t * UNITS + (U_UP + j + 1))
            for k in range(KD + 1):
                for j, b in ((0, k), (1, k - 1)):
                    if not 0 <= b < KD:
                        continue
                    if j == 0:
                        pe.wait_ge(*norm_act.at(f"hi{b}", t * 2 + 1))
                    pe.matmul(bank[j][:, :], w_hi[j][:, b, :], h_hi[:, b, :], start=b == 0, stop=False)
                    pe.matmul(bank[j][:, :], w_lo[j][:, b, :], h_hi[:, b, :], start=False, stop=False)
                    if j == 0:
                        pe.wait_ge(*norm_dve.at(f"lo{b}", t * 2 + 1))
                    mm = pe.matmul(bank[j][:, :], w_hi[j][:, b, :], h_lo[:, b, :], start=False, stop=b == KD - 1)
                    if b == KD - 1:
                        mm.then_inc(unit_done, 1)
            with pe.Fori(1, KF) as f:
                for j in range(2):
                    from_h(t, U_UP + j, f * 2, j, t * B_TILE + f + B_UP)

            def down(c, i, ready=None):
                j = c % 2
                for part in range(3):
                    a, b = DOWN_SPLIT[part], DOWN_SPLIT[part + 1]
                    if part == 2 and ready:
                        pe.wait_ge(*ready)
                    products(t, U_DOWN + 3 * c + part, i, bank[j][:, :], lambda k: g_hi[:, a + k, :],
                             lambda k: g_lo[:, a + k, :], b - a, first=part == 0, last=part == 2)

            pe.wait_ge(*up_dve.at("g_lo", t * KF + (KF - 2)))
            for c in range(KD):
                pe.wait_ge(evac[c % 2], t * B_TILE + (B_DOWN + c // 2))
                down(c, 0, up_dve.at("g_lo", t * KF + (KF - 1)) if c == 0 else None)
                if c == 3:
                    pe.wait_ge(*pre_dve.before((t + 1) * KD + KD))
                    token_sums(bank[2], sum_n).then_inc(*norm_pe.did("ssq"))
                if c == 4:
                    norm_spread(t * 2 + 2)
        pe.wait_ge(*res_dve.before(NT * 2 * KD))
        token_sums(bank[6], sum_r).then_inc(*fin_pe.did("ssq"))
        final_spread(NT)

    block.__exit__(None, None, None)


_ORDER = ("x_t", "w_units", "par", "masks_in", "ident_in", "gm_wt", "ln_b", "gm_bs")


def _columns(a):
    import numpy as np
    return np.asarray(a).reshape(-1, P).T


def _units(inputs):
    import numpy as np

    def unit(w, col, k0=0, k1=None):
        a = np.asarray(w)[k0 * P:None if k1 is None else k1 * P, col * P:(col + 1) * P]
        return a.reshape(-1, P, P).transpose(1, 0, 2)

    w_in, w_up, w_down = inputs["w_in"][0], inputs["w_up"][0], inputs["w_down"][0]
    u_at, v_at, q_at, f_at, i_at, og_at = (NH * n for n in range(6))
    ga_at, gb_at = 6 * NH, 6 * NH + KD
    out = np.zeros((UNITS + 2, P, KD, P), np.float32)
    n = 0
    for h in range(NH):
        for at in (f_at, q_at, i_at, og_at, v_at, u_at):
            out[n] = unit(w_in, at + h)
            n += 1
    for p in range(KD // 2):
        for j in range(2):
            c = 2 * p + j
            out[n + G_UNIT[p] + 2 * j] = unit(w_in, ga_at + c)
            out[n + G_UNIT[p] + 2 * j + 1] = unit(w_in, gb_at + c)
            out[n + B_UNIT[p] + j, :, :NH] = unit(inputs["w_br_hg"][0], c)
            out[n + B_UNIT[p] + j, :, NH:] = unit(inputs["w_br_gm"][0], c)
    n += 3 * KD
    for c in range(KD):
        out[n] = unit(inputs["w_out"][0], c)
        n += 1
    for f in range(KF):
        out[n], out[n + 1] = unit(w_up, f), unit(w_up, KF + f)
        n += 2
    for c in range(KD):
        for a, b in zip(DOWN_SPLIT, DOWN_SPLIT[1:]):
            out[n, :, :b - a] = unit(w_down, c, a, b)
            n += 1
    out[n:] = out[:2]
    return out


def _masks():
    import numpy as np
    j = np.arange(P)[:, None]
    parts = [np.tile(j == np.arange(P)[None], (1, NC))]
    for s in LEVELS:
        i = np.arange(P // 2)[None]
        parts.append(np.tile((j // (2 * s) == i // s) & (j % (2 * s) < s), (1, NC)))
    return np.concatenate(parts, axis=1).astype(np.uint32)


def kernel(**inputs):
    import numpy as np
    import concourse.bacc as bacc
    from concourse.bass_utils import run_bass_kernel_spmd

    inputs = {k: np.asarray(v) for k, v in inputs.items()}
    x_t = np.zeros((NT + 1, P, KD, TT), np.float32)
    x_t[:NT] = inputs["x"][0].reshape(NT, TT, KD, P).transpose(0, 3, 2, 1)
    par = np.zeros((P, N_PAR), np.float32)
    for at, a in ((C_MIXN, inputs["mix_norm"][0]), (C_FFNN, inputs["ffn_norm"][0]), (C_FINN, inputs["final_norm"]),
                  (C_LB, inputs["hg_lb_logits"][0]), (C_LNG, inputs["gm_ln_g"][0]), (C_HGN, inputs["hg_norm_g"][0]),
                  (C_CW, inputs["conv_w"][0]), (C_CB, inputs["conv_b"][0])):
        cols = _columns(a)
        par[:, at:at + cols.shape[1]] = cols
    arrays = {
        "x_t": x_t,
        "w_units": _units(inputs),
        "par": par,
        "masks_in": _masks(),
        "ident_in": np.eye(P, dtype=np.float32),
        "gm_wt": np.ascontiguousarray(inputs["gm_ws"][0].transpose(2, 0, 1)),
        "ln_b": np.ascontiguousarray(inputs["gm_ln_b"][0:1]),
        "gm_bs": np.ascontiguousarray(inputs["gm_bs"][0].reshape(1, NH * P)),
    }
    nc = bacc.Bacc("TRN2", target_bir_lowering=False, num_devices=1)
    args = [nc.dram_tensor(n, arrays[n].shape, mybir.dt.from_np(arrays[n].dtype), kind="ExternalInput").ap()
            for n in _ORDER]
    out = nc.dram_tensor("out", (NT + 1, P, KD, TT), F32, kind="ExternalOutput").ap()
    build(nc, *args, out)
    r = run_bass_kernel_spmd(nc, [arrays], core_ids=[0])
    got = r.results[0]["out"][1:]
    return np.ascontiguousarray(got.transpose(0, 3, 2, 1).reshape(1, SEQ, D))
```

```python
import concourse.bass as bass
from concourse import mybir

F32 = mybir.dt.float32
F32R = mybir.dt.float32r
U32 = mybir.dt.uint32
ACT = mybir.ActivationFunctionType
ALU = mybir.AluOpType

P = 128
D = 1024
SEQ = 2048
TT = 512
NT = SEQ // TT
NC = TT // P
KD = D // P
NH = 4
FF = 2816
KF = FF // P
EPS = 1e-6
TINY = 1e-30
LB_MAX = 0.999
LEVELS = [1, 2, 4, 8, 16, 32, 64]
GM_CHUNK = 64

U_TOK = 0
U_HEAD = U_TOK + KD
U_MIX = U_HEAD + 6 * NH
U_OUT = U_MIX + 2 * KD
U_UP = U_OUT + KD
U_DOWN = U_UP + 2 * KF
UNITS = U_DOWN + 3 * KD
DOWN_SPLIT = [0, 8, 15, KF]
I_BANKS = (2, 3, 0, 1)
B_TOK = 1
B_HEAD = B_TOK + 1
B_MIX = B_HEAD + 3 * NH
B_OUT = B_MIX + KD // 2
B_UP = B_OUT + KD // 2
B_DOWN = B_UP + KF
B_TILE = B_DOWN + KD // 2 - B_TOK

C_MIXN, C_FFNN, C_FINN = 0, KD, 2 * KD
C_LB = 3 * KD
C_LNG = C_LB + NH
C_HGN = C_LNG + NH
C_CW = C_HGN + 1
C_CB = C_CW + 3 * 2 * KF
N_PAR = C_CB + 2 * KF


class Steps:

    def __init__(self, sem, names, head_start=0):
        self.sem, self.names, self.n, self.head_start = sem, names, 0, head_start

    def did(self, name):
        assert self.names[self.n % len(self.names)] == name, (self.names[self.n % len(self.names)], name)
        self.n += 1
        return self.sem, 1

    def at(self, name, turn):
        return self.sem, turn * len(self.names) + (self.names.index(name) + 1 + self.head_start)

    def before(self, turn):
        return self.sem, turn * len(self.names) + self.head_start


def halves(ap, s):
    v = ap.rearrange("p (n two s) -> p n two s", two=2, s=s)
    return v[:, :, 0, :], v[:, :, 1, :]


def blocks(ap, s):
    return ap.rearrange("p (n s) -> p n s", s=s)


def spread(ap, s):
    return ap.unsqueeze(2).broadcast_to([P, ap.shape[1], s])


def build(nc, x_t, w_units, par, masks_in, ident_in, gm_wt, ln_b, gm_bs, out):
    top = [nc.sbuf_base + (-nc.sbuf_base) % 64]

    def place(name, shape, dt=F32, at=None):
        size = 4
        for n in shape[1:]:
            size *= n
        if at is None:
            at = top[0]
            top[0] += size + (-size) % 64
            assert top[0] <= nc.sbuf_usable_end, (name, top[0])
        return nc.alloc_sbuf_tensor_at(name, shape, dt, offset=at)

    def room(size):
        at = top[0]
        top[0] += size
        return at

    BLK = TT * 4
    raw = [place(f"raw{i}", [P, KD, P]) for i in range(2)]
    w_hi = [place(f"w_hi{i}", [P, KD, P], F32R) for i in range(2)]
    w_lo = [place(f"w_lo{i}", [P, KD, P], F32R) for i in range(2)]
    h_hi = place("h_hi", [P, KD, TT], F32R)
    at_lo = room(KD * BLK)
    h_lo = place("h_lo", [P, KD, TT], F32R, at_lo)
    x_in = place("x_in", [P, KD, TT], F32, at_lo)
    at_res = room(KD * BLK)
    res = place("res", [P, KD, TT], F32, at_res)
    gate_a_head = place("gate_a_head", [P, NH, TT], F32, at_res)
    gate_b_head = place("gate_b_head", [P, NH, TT], F32, at_res + NH * BLK)
    gate_a, gate_b = ([g[:, c, :] for c in range(NH)] for g in (gate_a_head, gate_b_head))
    carry = place("carry", [P, NH, P])
    state = place("state", [P, NC, P])
    halo = place("halo", [P, (NT + 1) * 2 * KF, 2])
    params = place("params", [P, N_PAR])
    lower = place("lower", [P, 4, NH])
    masks = place("masks", [P, NC * P + len(LEVELS) * NC * P // 2], U32)
    ident = place("ident", [P, P])
    ones = place("ones", [P, P])
    eps = place("eps", [P, 1])
    scratch = place("scratch", [P, 8])
    gm_w = place("gm_w", [P, NH, P])
    gm_b = place("gm_b", [P, NH, P])
    stats = place("stats", [P, NC, 6])
    moments = place("moments", [P, NC, 2])
    spreads = place("spreads", [P, 2, NC])
    tok_n = place("tok_n", [P, 2, NC])
    tok_r = place("tok_r", [P, 2, NC])
    tok_f = place("tok_f", [P, 2, NC])
    sum_r = place("sum_r", [P, TT])

    arena = room(2 * KF * BLK)
    g_hi = place("g_hi", [P, KF, TT], F32R, arena)
    g_lo = place("g_lo", [P, KF, TT], F32R, arena + KF * BLK)
    a_hi = place("a_hi", [P, NH, TT], F32R, arena)
    a_lo = place("a_lo", [P, NH, TT], F32R, arena + 4 * BLK)
    b_hi = place("b_hi", [P, NH, TT], F32R, arena + 8 * BLK)
    b_lo = place("b_lo", [P, NH, TT], F32R, arena + 12 * BLK)
    y_at = arena + 16 * BLK
    y_hi = place("y_hi", [P, KD, TT], F32R, y_at)
    y_lo = place("y_lo", [P, KD, TT], F32R, y_at + KD * BLK)
    q0 = place("q0", [P, TT], F32, y_at)
    qp = place("qp", [P, TT], F32, y_at + BLK)
    kp = {s: place(f"kp{s}", [P, TT], F32, y_at + (2 + n) * BLK)
          for n, s in enumerate(LEVELS + [P])}
    q_right = {s: place(f"qr{s}", [P, TT // 2], F32, y_at + 10 * BLK + n * BLK // 2)
               for n, s in enumerate(LEVELS)}
    t_at = y_at + 14 * BLK
    total = {}
    for s in LEVELS + [P]:
        total[s] = place(f"total{s}", [P, TT // s], F32, t_at)
        t_at += TT // s * 4
    assert t_at <= y_at + 16 * BLK
    u_act = place("u_act", [P, NH, TT], F32, y_at + 16 * BLK)
    v_tok = place("v_tok", [P, NC, NH * P], F32, y_at + 20 * BLK)
    late = y_at + 24 * BLK
    og_act = place("og_act", [P, TT], F32, late)
    head_o = place("head_o", [P, TT], F32, late + BLK)
    k_tok = place("k_tok", [P, TT], F32, late + 2 * BLK)
    scores = place("scores", [P, TT], F32, late + 3 * BLK)
    assert late + 4 * BLK <= arena + 2 * KF * BLK

    SLOT = BLK + 64
    pool = room(10 * SLOT)

    def temp(name, slot, width=TT):
        return place(name, [P, width], F32, pool + slot * SLOT)

    sig_f, sig_nf, sig_q, sig_og = (temp(n, i) for i, n in enumerate(("sig_f", "sig_nf", "sig_q", "sig_og")))
    gm_mix, v_head = temp("gm_mix", 4), temp("v_head", 5)
    i_tok = place("i_tok", [P, NC, NH * P], F32, pool + 6 * SLOT)
    i_head = place("i_head", [P, TT])
    sum_n, diag_n = temp("sum_n", 1), temp("diag_n", 3)
    h_f32 = [temp("h_f32a", 4), temp("h_f32b", 5)]
    sq_r, diag_r = temp("sq_r", 6), temp("diag_r", 7)
    rms_inv, diag_f = temp("rms_inv", 8), temp("diag_f", 9)
    conv = [temp("conv0", 0), temp("conv1", 1)]
    silu, g_f32 = temp("silu", 2), temp("g_f32", 3)
    z = [temp("z0", 4, TT + 2), temp("z1", 5, TT + 2)]
    for c in range(KD - NH):
        for n, gate in ((2 * c, gate_a), (2 * c + 1, gate_b)):
            at = pool + n * SLOT if n < 4 else late + (n - 4) * BLK
            gate.append(place(f"gate{n}", [P, TT], F32, at)[:, :])
    br_b, br_a, y_f32 = temp("br_b", 4), temp("br_a", 5), temp("y_f32", 6)
    lnb_row, bs_row = temp("lnb_row", 0), temp("bs_row", 2)

    bank = [nc.alloc_psum_tensor(f"bank{i}", [P, TT], F32) for i in range(8)]

    def sem(name):
        return nc.alloc_semaphore(name)

    par_in, consts_in, masks_here, res_in, out_sent = sem("par_in"), sem("consts_in"), sem("masks_here"), sem("res_in"), sem("out_sent")
    ident_here = sem("ident_here")
    x_next_in = [sem("x_next_in0"), sem("x_next_in1")]
    raw_in = [sem("raw_in0"), sem("raw_in1")]
    hi_made, lo_made, unit_done = sem("hi_made"), sem("lo_made"), sem("unit_done")
    evac = [sem("evac0"), sem("evac1")]
    N_CONST = 16 * 3

    tok_act = Steps(sem("tok_act"), ["i0", "i1"] + [f"v{c}" for c in range(NC)])
    head_act = Steps(sem("head_act"), ["i_head", "sig_f", "sig_q", "sig_og", "k_tok", "o_sq", "o_rms"])
    head_pe = Steps(sem("head_pe"), ["s1", "diag", "k_tok", "s64_32", "s16_8", "s4_2", "update", "o", "mix", "o_sum"])
    names = ["forget", "floor", "qp1"]
    for s in LEVELS:
        names += [f"qr{s}", f"qp{2 * s}", f"kl{2 * s}", f"kr{2 * s}", f"t{2 * s}"]
    head_dve = Steps(sem("head_dve"), ["k"] + names + [f"vh{c}" for c in range(NC)]
                     + ["m1", "m0", "m64", "m32", "m16", "m8", "m4", "m2", "st0", "st1", "st2", "st3", "st4",
                        "mix", "a", "a_hi", "a_lo", "inv", "unit", "b", "b_hi", "b_lo"])
    ln_dve = Steps(sem("ln_dve"), [f"bn{c}" for c in range(NC)] + [f"ag{c}" for c in range(NC)] + ["inv"])
    ln_act = Steps(sem("ln_act"), ["std"])
    mix_dve = Steps(sem("mix_dve"), [f"{n}{j}" for j in range(2) for n in ("b", "a", "y", "y_hi", "y_lo")], 1)
    out_act = Steps(sem("out_act"), ["sq0", "hi0", "sq1", "hi1"])
    out_dve = Steps(sem("out_dve"), [f"{n}{j}" for j in range(2) for n in ("f", "sum", "lo")], 1)
    ffn_pe, ffn_act = Steps(sem("ffn_pe"), ["ssq", "spread"]), Steps(sem("ffn_act"), ["rms", "inv"])
    ffn_dve = Steps(sem("ffn_dve"), ["inv", "diag"])
    res_act = Steps(sem("res_act"), ["sq"])
    res_dve = Steps(sem("res_dve"), ["sum"], 1)
    zero_dve = Steps(sem("zero_dve"), ["scores", "sum_out", "sum_down", "sum_n"])
    norm_pe = Steps(sem("norm_pe"), ["ssq", "spread"])
    norm_act = Steps(sem("norm_act"), ["rms"] + [f"hi{c}" for c in range(KD)])
    pre_act = Steps(sem("pre_act"), ["sq"])
    pre_dve = Steps(sem("pre_dve"), ["sum"], 1)
    names = ["inv", "diag", "f0"]
    for c in range(KD):
        names += ([f"f{c + 1}"] if c + 1 < KD else []) + [f"lo{c}"]
    norm_dve = Steps(sem("norm_dve"), names)
    up_act = Steps(sem("up_act"), ["silu"])
    up_dve = Steps(sem("up_dve"), [f"{n}{j}" for j in range(2) for n in ("in", "keep", "c", "d", "e")]
                   + ["g", "g_hi", "g_lo"], 1)
    fin_pe, fin_act = Steps(sem("fin_pe"), ["ssq", "spread"]), Steps(sem("fin_act"), ["rms"])
    fin_dve = Steps(sem("fin_dve"), ["inv", "diag"] + [f"o{c}" for c in range(KD)], 1)
    pro_dve, pro_act, pro_pe, pro_pool = sem("pro_dve"), sem("pro_act"), sem("pro_pe"), sem("pro_pool")

    def par_col(c, n=1):
        return params[:, c:c + n]

    def par_dyn(c, i):
        return params[:, bass.ds(c + i, 1)]

    mask_of, at = {0: masks[:, 0:TT]}, TT
    for s in LEVELS:
        mask_of[s] = masks[:, at:at + TT // 2]
        at += TT // 2
    level_place = {1: (3, 0), 64: (5, 0), 32: (5, 1), 16: (6, 0), 8: (6, 1), 4: (7, 0), 2: (7, 1)}

    def level_out(s):
        b, half = level_place[s]
        return bank[b][:, half * TT // 2:(half + 1) * TT // 2]

    block = nc.Block()
    block.__enter__()

    @block.sync
    def _(sp):
        def load(unit, slot):
            sp.dma_start(raw[slot][:, :, :], w_units[unit]).then_inc(raw_in[slot], 16)

        def stream(t, first, last):
            with sp.Fori(0, (last - first) // 2) as i:
                for j in range(2):
                    sp.wait_ge(lo_made, t * UNITS + i * 2 + (first + j + 1))
                    load(i * 2 + (first + j + 2), j)

        def load_x(tile):
            for j in range(2):
                part = slice(j * KD // 2, (j + 1) * KD // 2)
                sp.dma_start(x_in[:, part, :], x_t[tile, :, part, :]).then_inc(x_next_in[j], 16)

        sp.dma_start(params[:, :], par).then_inc(par_in, 16)
        load_x(0)
        sp.dma_start(ident[:, :], ident_in).then_inc(ident_here, 16)
        load(0, 0)
        load(1, 1)
        for a, b in ((gm_w[:, :, :], gm_wt), (lnb_row[:, :], ln_b.broadcast_to([P, NH * P])),
                     (bs_row[:, :], gm_bs.broadcast_to([P, NH * P]))):
            sp.dma_start(a, b).then_inc(consts_in, 16)
        sp.dma_start(masks[:, :], masks_in).then_inc(masks_here, 16)
        with sp.Fori(0, NT) as t:
            stream(t, 0, 6)
            sp.wait_ge(*fin_dve.before(t + 1))
            sp.dma_start(out[t], res[:, :, :]).then_inc(out_sent, 16)
            stream(t, 6, U_MIX + 10)
            sp.wait_ge(*mix_dve.at("a1", t * (KD // 2) + 1))
            sp.dma_start(res[:, :, :], x_t[t]).then_inc(res_in, 16)
            stream(t, U_MIX + 10, U_DOWN + 4)
            sp.wait_ge(unit_done, t * UNITS + U_DOWN)
            load_x(t + 1)
            stream(t, U_DOWN + 4, UNITS)
        for c in range(0, KD, 2):
            sp.wait_ge(*fin_dve.at(f"o{c + 1}", NT))
            sp.dma_start(out[NT, :, c:c + 2, :], res[:, c:c + 2, :]).then_inc(out_sent, 16)
        sp.wait_ge(out_sent, 16 * (NT + KD // 2))

    @block.gpsimd
    def _(po):
        po.memset(carry[:, :, :], 0.0).then_inc(pro_pool, 1)
        po.memset(halo[:, 0:2 * KF, :], 0.0).then_inc(pro_pool, 1)
        po.memset(res[:, :, :], 0.0).then_inc(pro_pool, 1)
        po.memset(sum_r[:, :], 0.0).then_inc(pro_pool, 1)
        po.wait_ge(consts_in, N_CONST)
        po.wait_ge(pro_pool, 4)
        po.memset(gm_w[GM_CHUNK:P, :, 0:GM_CHUNK], 0.0).then_inc(pro_pool, 1)
        po.wait_ge(pro_pool, 5)
        with po.Fori(0, (NT * UNITS + 2) // 2) as i:
            for j in range(2):
                po.wait_ge(hi_made, i * 2 + (j + 1))
                po.tensor_tensor(w_lo[j][:, :, :], raw[j][:, :, :], w_hi[j][:, :, :].bitcast(F32),
                                 ALU.subtract).then_inc(lo_made, 1)

    @block.scalar
    def _(act):
        def weights_hi(t, u, i=0):
            slot = u % 2
            act.wait_ge(unit_done, t * UNITS + i + (u + 1))
            act.wait_ge(raw_in[slot], t * (8 * UNITS) + i * 8 + 16 * (u // 2 + 2))
            act.activation(w_hi[slot][:, :, :], raw[slot][:, :, :], ACT.Copy).then_inc(hi_made, 1)

        def pre_square(turn, c):
            if c % (KD // 2) == 0:
                act.wait_ge(x_next_in[c // (KD // 2)], turn * 16 + 16)
            if c >= 2:
                act.wait_ge(*pre_dve.before(turn * KD + c - 1))
            act.activation(h_f32[c % 2][:, :], x_in[:, c, :], ACT.Square).then_inc(*pre_act.did("sq"))

        def norm_rms(turn):
            act.wait_ge(*norm_pe.at("ssq", turn))
            act.activation(tok_n[:, 0, :], bank[6][:, 0:NC], ACT.Sqrt, bias=eps[:, 0:1],
                           scale=1.0 / D).then_inc(*norm_act.did("rms"))

        def norm_hi(turn, a, b):
            for c in range(a, b):
                act.wait_ge(*norm_dve.at(f"f{c}", turn))
                act.activation(h_hi[:, c, :], h_f32[c % 2][:, :], ACT.Copy).then_inc(*norm_act.did(f"hi{c}"))

        act.wait_ge(pro_dve, 2)
        act.activation(lower[:, 1, :], lower[:, 0, :], ACT.Exp).then_inc(pro_act, 1)
        for c in range(KD):
            pre_square(0, c)
        for j in range(2):
            act.sem_inc(evac[j], 1)
            act.wait_ge(raw_in[j], 16)
            act.activation(w_hi[j][:, :, :], raw[j][:, :, :], ACT.Copy).then_inc(hi_made, 1)
        act.wait_ge(pro_dve, 1)
        norm_rms(0)
        norm_hi(0, 0, KD)
        act.wait_ge(pro_pool, 4)

        def final_rms(turn):
            act.wait_ge(*fin_pe.at("ssq", turn))
            act.activation(tok_r[:, 0, :], bank[4][:, 0:NC], ACT.Sqrt, bias=eps[:, 0:1],
                           scale=1.0 / D).then_inc(*fin_act.did("rms"))

        with act.Fori(0, NT) as t:
            for u in range(4):
                weights_hi(t, U_TOK + u)
                if u == 0:
                    final_rms(t)
            for c in range(NC):
                freed = (evac[I_BANKS[c]], 1) if c >= 2 else tok_act.did(f"i{c}")
                act.activation(i_tok[:, c, :], bank[I_BANKS[c]][:, :], ACT.Copy).then_inc(*freed)
            for u in range(4, 8):
                weights_hi(t, U_TOK + u)
            for c in range(NC):
                act.activation(v_tok[:, c, :], bank[4 + c][:, :], ACT.Gelu).then_inc(*tok_act.did(f"v{c}"))
            act.wait_ge(*ln_dve.at(f"ag{NC - 1}", t))
            act.activation(spreads[:, 0, :], moments[:, :, 1], ACT.Sqrt, bias=eps[:, 0:1]).then_inc(*ln_act.did("std"))
            act.wait_ge(pro_dve, 8)
            act.wait_ge(out_sent, t * 16 + 16)

            with act.Fori(0, NH) as h:
                it = t * NH + h
                u = h * 6
                act.activation(blocks(i_head[:, :], P), i_tok[:, :, bass.ts(h, P)],
                               ACT.Copy).then_inc(*head_act.did("i_head"))
                weights_hi(t, U_HEAD, u)
                act.activation(sig_f[:, :], bank[0][:, :], ACT.Sigmoid).then_inc(*head_act.did("sig_f"))
                act.activation(sig_nf[:, :], bank[0][:, :], ACT.Sigmoid, scale=-1.0).then_inc(evac[0], 1)
                weights_hi(t, U_HEAD + 1, u)
                act.activation(sig_q[:, :], bank[1][:, :], ACT.Sigmoid).then_inc(*head_act.did("sig_q"))
                weights_hi(t, U_HEAD + 2, u)
                act.activation(gate_a_head[:, h, :], bank[0][:, :], ACT.Sigmoid).then_inc(evac[0], 1)
                weights_hi(t, U_HEAD + 3, u)
                act.activation(sig_og[:, :], bank[1][:, :], ACT.Sigmoid).then_inc(*head_act.did("sig_og"))
                weights_hi(t, U_HEAD + 4, u)
                act.activation(gate_b_head[:, h, :], bank[0][:, :], ACT.Sigmoid).then_inc(evac[0], 1)
                act.wait_ge(*head_pe.at("k_tok", it))
                act.activation(k_tok[:, :], bank[2][:, :], ACT.Copy).then_inc(*head_act.did("k_tok"))
                weights_hi(t, U_HEAD + 5, u)
                act.activation(u_act[:, h, :], bank[1][:, :], ACT.Gelu).then_inc(evac[1], 1)
                act.wait_ge(*head_pe.at("o", it))
                act.activation(head_o[:, :], bank[4][:, :], ACT.Square).then_inc(*head_act.did("o_sq"))
                act.wait_ge(*head_pe.at("o_sum", it))
                act.activation(head_o[:, :], bank[5][:, :], ACT.Sqrt, bias=eps[:, 0:1],
                               scale=1.0 / P).then_inc(*head_act.did("o_rms"))

            for p in range(KD // 2):
                weights_hi(t, U_MIX + 4 * p)
                act.activation(gate_a[NH + p], bank[0][:, :], ACT.Sigmoid).then_inc(evac[0], 1)
                weights_hi(t, U_MIX + 4 * p + 1)
                act.activation(gate_b[NH + p], bank[1][:, :], ACT.Sigmoid).then_inc(evac[1], 1)
                for j in range(2):
                    weights_hi(t, U_MIX + 4 * p + 2 + j)

            with act.Fori(0, KD // 2) as p:
                it = t * (KD // 2) + p
                for j in range(2):
                    weights_hi(t, U_OUT + j, p * 2)
                    act.wait_ge(evac[j], t * B_TILE + p + (B_OUT + 1))
                    if j == 0:
                        act.wait_ge(*out_dve.before(it))
                    else:
                        act.wait_ge(*out_dve.at("sum0", it))
                    act.activation(sq_r[:, :], res[:, p * 2 + j, :],
                                   ACT.Square).then_inc(*out_act.did(f"sq{j}"))
                    act.wait_ge(*out_dve.at(f"f{j}", it))
                    act.activation(h_hi[:, p * 2 + j, :], h_f32[j][:, :], ACT.Copy).then_inc(*out_act.did(f"hi{j}"))

            weights_hi(t, U_UP)
            act.wait_ge(*ffn_pe.at("ssq", t))
            act.activation(tok_f[:, 0, :], bank[4][:, 0:NC], ACT.Sqrt, bias=eps[:, 0:1],
                           scale=1.0 / D).then_inc(*ffn_act.did("rms"))
            act.wait_ge(*ffn_pe.at("spread", t))
            act.activation(rms_inv[:, :], bank[5][:, :], ACT.Copy).then_inc(*ffn_act.did("inv"))
            weights_hi(t, U_UP + 1)
            act.wait_ge(*up_dve.at("e0", t * KF))
            act.activation(silu[:, :], conv[0][:, :], ACT.Silu).then_inc(*up_act.did("silu"))
            with act.Fori(1, KF) as f:
                for j in range(2):
                    weights_hi(t, U_UP + j, f * 2)
                act.wait_ge(*up_dve.at("e0", t * KF + f))
                act.activation(silu[:, :], conv[0][:, :], ACT.Silu).then_inc(*up_act.did("silu"))

            for p in range(KD // 2):
                for j in range(2):
                    for part in range(3):
                        weights_hi(t, U_DOWN + 6 * p + 3 * j + part)
                        if p == 1 and part < 2:
                            for c in range(4 * j + 2 * part, 4 * j + 2 * part + 2):
                                pre_square(t + 1, c)
                        if p == 2 and j == 0 and part == 0:
                            norm_rms(t + 1)
                        if (p, j) in ((2, 1), (3, 0)) and part < 2:
                            norm_hi(t + 1, 4 * (p - 2) + 2 * part, 4 * (p - 2) + 2 * part + 2)
                    c = 2 * p + j
                    act.wait_ge(evac[j], t * B_TILE + (B_DOWN + p + 1))
                    act.wait_ge(*res_dve.before(t * KD + c))
                    act.activation(sq_r[:, :], res[:, c, :], ACT.Square).then_inc(*res_act.did("sq"))
        final_rms(NT)

    @block.vector
    def _(dve):
        def inverse(tok, diag, steps, turn):
            dve.reciprocal(tok[:, 1, :], tok[:, 0, :]).then_inc(*steps.did("inv"))
            dve.wait_ge(*steps.at("inv", turn))
            dve.tensor_tensor(blocks(diag[:, :], P), ident[:, :].unsqueeze(1).broadcast_to([P, NC, P]),
                              spread(tok[:, 1, :], P), ALU.mult).then_inc(*steps.did("diag"))

        def pre_sum(turn, c):
            dve.wait_ge(*pre_act.at("sq", turn * KD + c))
            dve.wait_ge(*pre_dve.before(turn * KD + c))
            dve.tensor_tensor(sum_n[:, :], sum_n[:, :], h_f32[c % 2][:, :], ALU.add).then_inc(*pre_dve.did("sum"))

        def norm_inv(turn):
            dve.wait_ge(*norm_act.at("rms", turn))
            inverse(tok_n, diag_n, norm_dve, turn)

        def norm_parts(turn, src, col, a, b):
            def whole(c):
                if c == 0:
                    dve.wait_ge(*norm_pe.at("spread", turn))
                else:
                    dve.wait_ge(*norm_dve.at(f"lo{c - 2}" if c > 1 else "diag", turn))
                dve.scalar_tensor_tensor(out=h_f32[c % 2][:, :], in0=src[:, c, :], scalar=par_col(col + c),
                                         in1=bank[7][:, :], op0=ALU.mult, op1=ALU.mult).then_inc(*norm_dve.did(f"f{c}"))
            if a == 0:
                whole(0)
            for c in range(a, b):
                if c + 1 < KD:
                    whole(c + 1)
                dve.wait_ge(*norm_act.at(f"hi{c}", turn))
                dve.tensor_tensor(h_lo[:, c, :], h_f32[c % 2][:, :], h_hi[:, c, :].bitcast(F32),
                                  ALU.subtract).then_inc(*norm_dve.did(f"lo{c}"))

        for steps in (mix_dve, out_dve, res_dve, pre_dve, up_dve, fin_dve):
            dve.sem_inc(steps.sem, steps.head_start)
        dve.memset(sum_n[:, :], 0.0)
        dve.memset(ones[:, :], 1.0)
        dve.memset(eps[:, :], EPS).then_inc(pro_dve, 1)
        dve.wait_ge(pro_dve, 1)
        dve.wait_ge(par_in, 16)
        lb = par_col(C_LB, NH)
        dve.tensor_tensor(lower[:, 0, :], lb, lb, ALU.subtract).then_inc(pro_dve, 1)
        dve.wait_ge(pro_act, 1)
        dve.reciprocal(lower[:, 2, :], lower[:, 1, :]).then_inc(pro_dve, 1)
        dve.wait_ge(pro_dve, 3)
        dve.tensor_tensor(lower[:, 3, :], lower[:, 1, :], lower[:, 2, :], ALU.mult).then_inc(pro_dve, 1)
        dve.wait_ge(pro_dve, 4)
        dve.tensor_tensor(lower[:, 1, :], lower[:, 3, :], lower[:, 3, :], ALU.subtract).then_inc(pro_dve, 1)
        dve.wait_ge(pro_dve, 5)
        dve.tensor_scalar(lower[:, 2, :], lower[:, 1, :], 0.0, LB_MAX, ALU.max, ALU.min).then_inc(pro_dve, 1)
        dve.wait_ge(pro_dve, 6)
        dve.tensor_scalar(lower[:, 3, :], lower[:, 2, :], -1.0, 1.0, ALU.mult, ALU.add).then_inc(pro_dve, 1)
        for c in range(KD):
            pre_sum(0, c)
        dve.wait_ge(ident_here, 16)
        norm_inv(0)
        norm_parts(0, x_in, C_MIXN, 0, KD)
        dve.wait_ge(consts_in, N_CONST)
        dve.wait_ge(pro_pe, 1)
        dve.tensor_tensor(gm_b[:, :, :], blocks(bank[6][:, :], P), blocks(bs_row[:, :], P), ALU.add).then_inc(pro_dve, 1)
        dve.wait_ge(pro_pool, 4)
        dve.wait_ge(masks_here, 16)
        dve.wait_ge(pro_dve, 8)

        def final_out(turn):
            dve.wait_ge(*fin_act.at("rms", turn))
            inverse(tok_r, diag_r, fin_dve, turn)
            dve.wait_ge(*fin_pe.at("spread", turn))
            for c in range(KD):
                dve.scalar_tensor_tensor(out=res[:, c, :], in0=res[:, c, :], scalar=par_col(C_FINN + c),
                                         in1=bank[5][:, :], op0=ALU.mult,
                                         op1=ALU.mult).then_inc(*fin_dve.did(f"o{c}"))

        with dve.Fori(0, NT) as t:
            dve.memset(scores[:, :], 0.0).then_inc(*zero_dve.did("scores"))
            final_out(t)

            for c in range(NC):
                dve.wait_ge(*tok_act.at(f"v{c}", t))
                dve.bn_stats(out=stats[:, c, :], in_=v_tok[:, c, :]).then_inc(*ln_dve.did(f"bn{c}"))
            dve.wait_ge(*ln_dve.at(f"bn{NC - 1}", t))
            dve.memset(scratch[:, 0:1], 0.0)
            for c in range(NC):
                dve.bn_aggr(out=moments[:, c, :], in_=stats[:, c, :]).then_inc(*ln_dve.did(f"ag{c}"))
            dve.wait_ge(*ln_act.at("std", t))
            dve.reciprocal(spreads[:, 1, :], spreads[:, 0, :]).then_inc(*ln_dve.did("inv"))

            with dve.Fori(0, NH) as h:
                it = t * NH + h
                used = t * B_TILE + h * 3 + B_HEAD
                keep = lower[:, 3, bass.ds(h, 1)]

                def then(name):
                    dve.wait_ge(*head_dve.at(name, it))

                dve.wait_ge(evac[0], used + 1)
                dve.tensor_scalar(kp[1][:, :], sig_nf[:, :], keep, None, ALU.mult).then_inc(*head_dve.did("k"))
                dve.wait_ge(*head_act.at("sig_f", it))
                dve.tensor_scalar(total[1][:, :], sig_f[:, :], keep, lower[:, 2, bass.ds(h, 1)], ALU.mult,
                                  ALU.add).then_inc(*head_dve.did("forget"))
                then("forget")
                dve.tensor_scalar(total[1][:, :], total[1][:, :], TINY, None, ALU.max).then_inc(*head_dve.did("floor"))
                dve.wait_ge(*head_act.at("sig_q", it))
                dve.tensor_tensor(q0[:, :], sig_q[:, :], bank[1][:, :], ALU.mult).then_inc(evac[1], 1)
                then("floor")
                dve.wait_ge(evac[1], used + 1)
                dve.tensor_tensor(qp[:, :], q0[:, :], total[1][:, :], ALU.mult).then_inc(*head_dve.did("qp1"))
                for s in LEVELS:
                    then(f"t{s}" if s > 1 else "qp1")
                    q_l, q_r = halves(qp[:, :], s)
                    k_l, k_r = halves(kp[s][:, :], s)
                    k2_l, k2_r = halves(kp[2 * s][:, :], s)
                    t_l, t_r = halves(total[s][:, :], 1)
                    t_l, t_r = t_l[:, :, 0], t_r[:, :, 0]
                    dve.tensor_copy(blocks(q_right[s][:, :], s), q_r).then_inc(*head_dve.did(f"qr{s}"))
                    then(f"qr{s}")
                    dve.tensor_tensor(q_r, blocks(q_right[s][:, :], s), spread(t_l, s),
                                      ALU.mult).then_inc(*head_dve.did(f"qp{2 * s}"))
                    dve.tensor_tensor(k2_l, k_l, spread(t_r, s), ALU.mult).then_inc(*head_dve.did(f"kl{2 * s}"))
                    dve.tensor_copy(k2_r, k_r).then_inc(*head_dve.did(f"kr{2 * s}"))
                    dve.tensor_tensor(total[2 * s][:, :], t_l, t_r, ALU.mult).then_inc(*head_dve.did(f"t{2 * s}"))
                dve.wait_ge(*head_act.at("sig_og", it))
                dve.tensor_tensor(og_act[:, :], sig_og[:, :], bank[1][:, :], ALU.mult).then_inc(evac[1], 1)

                dve.wait_ge(*ln_dve.at("inv", t))
                for c in range(NC):
                    dve.tensor_scalar(v_head[:, c * P:(c + 1) * P], v_tok[:, c, bass.ts(h, P)], moments[:, c, 0:1],
                                      spreads[:, 1, c:c + 1], ALU.subtract, ALU.mult).then_inc(*head_dve.did(f"vh{c}"))

                for n, (s, made, before) in enumerate(((1, "s1", f"t{P}"), (0, "diag", "m1"), (64, "s64_32", "m0"),
                                                       (32, "s64_32", "m64"), (16, "s16_8", "m32"),
                                                       (8, "s16_8", "m16"), (4, "s4_2", "m8"), (2, "s4_2", "m4"))):
                    dve.wait_ge(*zero_dve.at("scores", t))
                    dve.wait_ge(*head_pe.at(made, it))
                    then(before)
                    dve.memset(scratch[:, n:n + 1], 0.0)
                    rows = P // 2 if s == P // 2 else P
                    if s:
                        dve.copy_predicated(halves(scores[0:rows, :], s)[1], blocks(mask_of[s][0:rows, :], s),
                                            blocks(level_out(s)[0:rows, :], s)).then_inc(*head_dve.did(f"m{s}"))
                    else:
                        dve.copy_predicated(scores[:, :], mask_of[0], bank[4][:, :]).then_inc(*head_dve.did("m0"))
                dve.tensor_copy(state[:, 0, :], carry[:, h, :]).then_inc(*head_dve.did("st0"))
                dve.wait_ge(*head_pe.at("update", it))
                for c in range(NC):
                    then(f"st{c}")
                    dve.scalar_tensor_tensor(out=state[:, c + 1, :] if c + 1 < NC else carry[:, h, :],
                                             in0=state[:, c, :], scalar=total[P][:, c:c + 1],
                                             in1=bank[2][:, c * P:(c + 1) * P], op0=ALU.mult,
                                             op1=ALU.add).then_inc(*head_dve.did(f"st{c + 1}"))
                dve.wait_ge(*head_pe.at("mix", it))
                dve.scalar_tensor_tensor(out=blocks(gm_mix[:, :], P), in0=blocks(bank[3][:, :], P),
                                         scalar=par_dyn(C_LNG, h),
                                         in1=gm_b[:, bass.ds(h, 1), :].broadcast_to([P, NC, P]),
                                         op0=ALU.mult, op1=ALU.add).then_inc(*head_dve.did("mix"))
                then("mix")
                dve.wait_ge(evac[1], used + 3)
                dve.tensor_tensor(gm_mix[:, :], gm_mix[:, :], u_act[:, h, :], ALU.mult).then_inc(*head_dve.did("a"))
                then("a")
                dve.tensor_scalar(a_hi[:, h, :], gm_mix[:, :], 1.0, None, ALU.mult).then_inc(*head_dve.did("a_hi"))
                then("a_hi")
                dve.tensor_tensor(a_lo[:, h, :], gm_mix[:, :], a_hi[:, h, :].bitcast(F32),
                                  ALU.subtract).then_inc(*head_dve.did("a_lo"))
                dve.wait_ge(*head_act.at("o_rms", it))
                dve.reciprocal(head_o[:, :], head_o[:, :]).then_inc(*head_dve.did("inv"))
                then("inv")
                dve.tensor_tensor(head_o[:, :], head_o[:, :], bank[4][:, :], ALU.mult).then_inc(*head_dve.did("unit"))
                then("unit")
                dve.scalar_tensor_tensor(out=head_o[:, :], in0=head_o[:, :], scalar=par_col(C_HGN), in1=og_act[:, :],
                                         op0=ALU.mult, op1=ALU.mult).then_inc(*head_dve.did("b"))
                then("b")
                dve.tensor_scalar(b_hi[:, h, :], head_o[:, :], 1.0, None, ALU.mult).then_inc(*head_dve.did("b_hi"))
                then("b_hi")
                dve.tensor_tensor(b_lo[:, h, :], head_o[:, :], b_hi[:, h, :].bitcast(F32),
                                  ALU.subtract).then_inc(*head_dve.did("b_lo"))

            dve.wait_ge(evac[0], t * B_TILE + B_MIX)
            for c in range(KD):
                p, j = c // 2, c % 2

                def then(name):
                    dve.wait_ge(*mix_dve.at(name, t * (KD // 2) + p))

                if c >= NH:
                    dve.wait_ge(evac[1], t * B_TILE + (B_MIX + c - NH + 1))
                dve.wait_ge(unit_done, t * UNITS + (U_MIX + 4 * p + 2 + j + 1))
                dve.tensor_tensor(br_b[:, :], gate_b[c], bank[4 + j][:, :],
                                  ALU.mult).then_inc(*mix_dve.did(f"b{j}"))
                dve.tensor_tensor(br_a[:, :], gate_a[c], bank[6 + j][:, :],
                                  ALU.mult).then_inc(*mix_dve.did(f"a{j}"))
                then(f"a{j}")
                dve.tensor_tensor(y_f32[:, :], br_a[:, :], br_b[:, :], ALU.add).then_inc(*mix_dve.did(f"y{j}"))
                then(f"y{j}")
                dve.tensor_copy(y_hi[:, c, :], y_f32[:, :]).then_inc(*mix_dve.did(f"y_hi{j}"))
                then(f"y_hi{j}")
                dve.tensor_tensor(y_lo[:, c, :], y_f32[:, :], y_hi[:, c, :].bitcast(F32),
                                  ALU.subtract).then_inc(*mix_dve.did(f"y_lo{j}"))

            dve.memset(sum_r[:, :], 0.0).then_inc(*zero_dve.did("sum_out"))
            with dve.Fori(0, KD // 2) as p:
                dve.wait_ge(*zero_dve.at("sum_out", t))
                dve.wait_ge(res_in, t * 16 + 16)
                it = t * (KD // 2) + p
                for j in range(2):
                    c = p * 2 + j
                    dve.wait_ge(unit_done, t * UNITS + p * 2 + (U_OUT + j + 1))
                    dve.tensor_tensor(res[:, c, :], res[:, c, :], bank[j][:, :], ALU.add).then_inc(evac[j], 1)
                    dve.wait_ge(evac[j], t * B_TILE + p + (B_OUT + 1))
                    dve.wait_ge(*out_dve.before(it))
                    dve.tensor_scalar(h_f32[j][:, :], res[:, c, :], par_dyn(C_FFNN + j, p * 2), None,
                                      ALU.mult).then_inc(*out_dve.did(f"f{j}"))
                    dve.wait_ge(*out_act.at(f"sq{j}", it))
                    if j == 1:
                        dve.wait_ge(*out_dve.at("sum0", it))
                    dve.tensor_tensor(sum_r[:, :], sum_r[:, :], sq_r[:, :], ALU.add).then_inc(*out_dve.did(f"sum{j}"))
                    dve.wait_ge(*out_act.at(f"hi{j}", it))
                    dve.tensor_tensor(h_lo[:, c, :], h_f32[j][:, :], h_hi[:, c, :].bitcast(F32),
                                      ALU.subtract).then_inc(*out_dve.did(f"lo{j}"))
            dve.wait_ge(*out_dve.before((t + 1) * (KD // 2)))
            dve.wait_ge(*ffn_act.at("rms", t))
            inverse(tok_f, diag_f, ffn_dve, t)

            with dve.Fori(0, KF) as f:
                it = t * KF + f

                def then(name):
                    dve.wait_ge(*up_dve.at(name, it))

                for j in range(2):
                    ch = f + j * KF
                    col = t * (2 * KF) + f + j * KF
                    dve.wait_ge(unit_done, t * UNITS + f * 2 + (U_UP + j + 1))
                    dve.wait_ge(*ffn_act.at("inv", t))
                    dve.wait_ge(*up_dve.before(it))
                    dve.tensor_tensor(z[j][:, 2:TT + 2], bank[j][:, :], rms_inv[:, :], ALU.mult).then_inc(evac[j], 1)
                    dve.tensor_scalar(z[j][:, 0:2], halo[:, col, :], 1.0, None, ALU.mult).then_inc(*up_dve.did(f"in{j}"))
                    dve.wait_ge(evac[j], t * B_TILE + f + (B_UP + 1))
                    dve.tensor_scalar(halo[:, col + 2 * KF, :], z[j][:, TT:TT + 2], 1.0, None,
                                      ALU.mult).then_inc(*up_dve.did(f"keep{j}"))
                    dve.tensor_scalar(conv[j][:, :], z[j][:, 2:TT + 2], par_dyn(C_CW + 4 * KF, ch), par_dyn(C_CB, ch),
                                      ALU.mult, ALU.add).then_inc(*up_dve.did(f"c{j}"))
                    for tap, name, before in ((1, "d", "c"), (0, "e", "d")):
                        then(f"{before}{j}")
                        dve.scalar_tensor_tensor(out=conv[j][:, :], in0=z[j][:, tap:TT + tap],
                                                 scalar=par_dyn(C_CW + 2 * KF * tap, ch), in1=conv[j][:, :],
                                                 op0=ALU.mult, op1=ALU.add).then_inc(*up_dve.did(f"{name}{j}"))
                dve.wait_ge(*up_act.at("silu", it))
                then("e1")
                dve.tensor_tensor(g_f32[:, :], silu[:, :], conv[1][:, :], ALU.mult).then_inc(*up_dve.did("g"))
                then("g")
                dve.tensor_scalar(g_hi[:, f, :], g_f32[:, :], 1.0, None, ALU.mult).then_inc(*up_dve.did("g_hi"))
                then("g_hi")
                dve.tensor_tensor(g_lo[:, f, :], g_f32[:, :], g_hi[:, f, :].bitcast(F32),
                                  ALU.subtract).then_inc(*up_dve.did("g_lo"))

            dve.memset(sum_r[:, :], 0.0).then_inc(*zero_dve.did("sum_down"))
            dve.memset(sum_n[:, :], 0.0).then_inc(*zero_dve.did("sum_n"))
            dve.wait_ge(*zero_dve.at("sum_n", t))
            for p in range(KD // 2):
                if p == 2:
                    norm_inv(t + 1)
                for j in range(2):
                    if (p, j) in ((2, 1), (3, 0)):
                        norm_parts(t + 1, x_in, C_MIXN, 4 * (p - 2), 4 * (p - 1))
                    if p == 1:
                        for c in range(4 * j, 4 * j + 4):
                            pre_sum(t + 1, c)
                    c = 2 * p + j
                    dve.wait_ge(unit_done, t * UNITS + (U_DOWN + 3 * c + 3))
                    dve.tensor_tensor(res[:, c, :], res[:, c, :], bank[j][:, :], ALU.add).then_inc(evac[j], 1)
                    dve.wait_ge(*res_act.at("sq", t * KD + c))
                    if c:
                        dve.wait_ge(*res_dve.before(t * KD + c))
                    dve.tensor_tensor(sum_r[:, :], sum_r[:, :], sq_r[:, :], ALU.add).then_inc(*res_dve.did("sum"))
        final_out(NT)

    @block.tensor
    def _(pe):
        def products(t, u, i, dst, rhs_hi, rhs_lo, n, first=True, last=True, off=0, ready=None, done=True):
            slot = u % 2
            if ready is None:
                pe.wait_ge(hi_made, t * UNITS + i + (u + 1))
                for k in range(n):
                    pe.matmul(dst, w_hi[slot][:, off + k, :], rhs_hi(k), start=first and k == 0, stop=False)
                    pe.matmul(dst, w_hi[slot][:, off + k, :], rhs_lo(k), start=False, stop=False)
                pe.wait_ge(lo_made, t * UNITS + i + (u + 1))
                for k in range(n):
                    mm = pe.matmul(dst, w_lo[slot][:, off + k, :], rhs_hi(k), start=False, stop=last and k == n - 1)
            else:
                pe.wait_ge(lo_made, t * UNITS + i + (u + 1))
                for k in range(n):
                    pe.wait_ge(*ready[0](k))
                    pe.matmul(dst, w_hi[slot][:, off + k, :], rhs_hi(k), start=first and k == 0, stop=False)
                    pe.matmul(dst, w_lo[slot][:, off + k, :], rhs_hi(k), start=False, stop=False)
                    pe.wait_ge(*ready[1](k))
                    mm = pe.matmul(dst, w_hi[slot][:, off + k, :], rhs_lo(k), start=False, stop=last and k == n - 1)
            if done:
                mm.then_inc(unit_done, 1)

        def from_h(t, u, i, b, uses, ready=None):
            pe.wait_ge(evac[b], uses)
            products(t, u, i, bank[b][:, :], lambda k: h_hi[:, k, :], lambda k: h_lo[:, k, :], KD, ready=ready)

        def token_sums(dst, sums):
            for c in range(NC):
                mm = pe.matmul(dst[:, c:c + 1], sums[:, c * P:(c + 1) * P], ones[:, 0:1], start=True, stop=True)
            return mm

        def norm_spread(dst, diag, dve_steps, pe_steps, turn):
            pe.wait_ge(*dve_steps.at("diag", turn))
            pe.matmul(dst[:, :], ones[:, :], diag[:, :], start=True, stop=True).then_inc(*pe_steps.did("spread"))

        def for_tokens(t, n, dst, is_i):
            u, slot = U_TOK + n, n % 2
            n %= 4
            pe.wait_ge(lo_made, t * UNITS + (u + 1))
            for k in range(2 * n, 2 * n + 2):
                cols = slice((k % 2) * NC, (k % 2 + 1) * NC)
                w = [w_hi[slot][:, cols, :], w_lo[slot][:, cols, :]]
                if is_i:
                    pe.wait_ge(*norm_act.at(f"hi{k}", t))
                    pe.wait_ge(*norm_dve.at(f"lo{k}", t))
                for c in range(NC):
                    tok = slice(c * P, (c + 1) * P)
                    if is_i and k == 0 and c >= 2:
                        pe.wait_ge(evac[I_BANKS[c]], t * B_TILE + B_TOK)
                    pe.matmul(dst[c][:, :], h_hi[:, k, tok], w[0], start=k == 0, stop=False)
                    pe.matmul(dst[c][:, :], h_hi[:, k, tok], w[1], start=False, stop=False)
                    mm = pe.matmul(dst[c][:, :], h_lo[:, k, tok], w[0], start=False, stop=k == KD - 1)
            mm.then_inc(unit_done, 1)

        def flip(dst, src):
            for c in range(NC):
                mm = pe.transpose(dst[:, c * P:(c + 1) * P], src[:, c * P:(c + 1) * P], ident[:, :])
            return mm

        def level(s):
            dst, rows = level_out(s), P // 2 if s == P // 2 else P
            for c in range(NC):
                mm = pe.matmul(dst[0:rows, c * P // 2:(c + 1) * P // 2], kp[s][:, c * P:c * P + rows],
                               q_right[s][:, c * P // 2:(c + 1) * P // 2], start=True, stop=True)
            return mm

        pe.wait_ge(*pre_dve.at("sum", KD - 1))
        token_sums(bank[6], sum_n).then_inc(*norm_pe.did("ssq"))
        norm_spread(bank[7], diag_n, norm_dve, norm_pe, 0)
        pe.wait_ge(pro_pool, 5)
        for h in range(NH):
            mm = pe.matmul(bank[6][:, h * P:(h + 1) * P], lnb_row[:, h * P:(h + 1) * P], gm_w[:, h, :],
                           start=True, stop=True)
        mm.then_inc(pro_pe, 1)

        with pe.Fori(0, NT) as t:
            for n in range(4):
                for_tokens(t, n, [bank[b] for b in I_BANKS], True)
                if n == 0:
                    pe.wait_ge(*res_dve.before(t * KD))
                    token_sums(bank[4], sum_r).then_inc(*fin_pe.did("ssq"))
                if n == 1:
                    norm_spread(bank[5], diag_r, fin_dve, fin_pe, t)
            pe.wait_ge(pro_dve, 8)
            pe.wait_ge(*fin_dve.before(t + 1))
            for n in range(4, 8):
                for_tokens(t, n, bank[4:8], False)

            with pe.Fori(0, NH) as h:
                it = t * NH + h
                u = h * 6
                used = t * B_TILE + h * 3 + B_HEAD
                from_h(t, U_HEAD, u, 0, used)
                from_h(t, U_HEAD + 1, u, 1, used)
                from_h(t, U_HEAD + 2, u, 0, used + 1)
                from_h(t, U_HEAD + 3, u, 1, used + 1)
                pe.wait_ge(*tok_act.at(f"v{NC - 1}", t))
                pe.wait_ge(*head_dve.at("qr1", it))
                level(1).then_inc(*head_pe.did("s1"))
                for c in range(NC):
                    cols = slice(c * P, (c + 1) * P)
                    mm = pe.matmul(bank[4][:, cols], kp[1][:, cols], q0[:, cols], start=True, stop=True)
                mm.then_inc(*head_pe.did("diag"))
                from_h(t, U_HEAD + 4, u, 0, used + 2)
                pe.wait_ge(*head_dve.at(f"t{P}", it))
                flip(bank[2], kp[P]).then_inc(*head_pe.did("k_tok"))
                for a, b in ((64, 32), (16, 8), (4, 2)):
                    level(a)
                    level(b).then_inc(*head_pe.did(f"s{a}_{b}"))
                from_h(t, U_HEAD + 5, u, 1, used + 2)
                pe.wait_ge(*head_dve.at("m2", it))
                pe.wait_ge(*head_act.at("k_tok", it))
                pe.wait_ge(*head_act.at("i_head", it))
                for c in range(NC):
                    cols = slice(c * P, (c + 1) * P)
                    mm = pe.matmul(bank[2][:, cols], k_tok[:, cols], i_head[:, cols], start=True, stop=True)
                mm.then_inc(*head_pe.did("update"))
                for c in range(NC):
                    cols = slice(c * P, (c + 1) * P)
                    pe.matmul(bank[4][:, cols], i_head[:, cols], scores[:, cols], start=True, stop=False)
                    pe.wait_ge(*head_dve.at(f"st{c}", it))
                    mm = pe.matmul(bank[4][:, cols], state[:, c, :], qp[:, cols], start=False, stop=True)
                mm.then_inc(*head_pe.did("o"))
                for c in range(NC):
                    cols = slice(c * P, (c + 1) * P)
                    mm = pe.matmul(bank[3][:, cols], v_head[:, cols], gm_w[:, h, :], start=True, stop=True)
                mm.then_inc(*head_pe.did("mix"))
                pe.wait_ge(*head_act.at("o_sq", it))
                pe.matmul(bank[5][:, :], ones[:, :], head_o[:, :], start=True,
                          stop=True).then_inc(*head_pe.did("o_sum"))

            def gates(u, uses):
                for j in range(2):
                    from_h(t, U_MIX + j, u, j, uses)

            def branches(j, u):
                products(t, U_MIX + 2 + j, u, bank[4 + j][:, :], lambda k: b_hi[:, k, :],
                         lambda k: b_lo[:, k, :], NH, done=False)
                products(t, U_MIX + 2 + j, u, bank[6 + j][:, :], lambda k: a_hi[:, k, :],
                         lambda k: a_lo[:, k, :], NH, off=NH)

            gates(0, t * B_TILE + B_MIX)
            pe.wait_ge(*head_dve.at("b_lo", t * NH + (NH - 1)))
            for j in range(2):
                branches(j, 0)
            with pe.Fori(1, KD // 2) as p:
                gates(p * 4, t * B_TILE + p + B_MIX)
                for j in range(2):
                    pe.wait_ge(*mix_dve.at(f"a{j}", t * (KD // 2) + p - 1))
                    branches(j, p * 4)

            def project(i, uses, ready=None):
                for j in range(2):
                    pe.wait_ge(evac[j], uses)
                    products(t, U_OUT + j, i, bank[j][:, :], lambda k: y_hi[:, k, :], lambda k: y_lo[:, k, :], KD,
                             ready=ready if j == 0 else None)

            project(0, t * B_TILE + B_OUT, (lambda k: mix_dve.at(f"y_hi{k % 2}", t * (KD // 2) + k // 2),
                                            lambda k: mix_dve.at(f"y_lo{k % 2}", t * (KD // 2) + k // 2)))
            with pe.Fori(1, KD // 2) as p:
                project(p * 2, t * B_TILE + p + B_OUT)
            def pair(k):
                return t * (KD // 2) + k // 2

            from_h(t, U_UP, 0, 0, t * B_TILE + B_UP, (lambda k: out_act.at(f"hi{k % 2}", pair(k)),
                                                      lambda k: out_dve.at(f"lo{k % 2}", pair(k))))
            token_sums(bank[4], sum_r).then_inc(*ffn_pe.did("ssq"))
            pe.wait_ge(evac[1], t * B_TILE + B_UP)
            for n in range(2):
                at = n * KD // 2
                products(t, U_UP + 1, 0, bank[1][:, :], lambda k: h_hi[:, at + k, :], lambda k: h_lo[:, at + k, :],
                         KD // 2, first=n == 0, last=n == 1, off=at, done=n == 1)
                if n == 0:
                    norm_spread(bank[5], diag_f, ffn_dve, ffn_pe, t)
            with pe.Fori(1, KF) as f:
                for j in range(2):
                    from_h(t, U_UP + j, f * 2, j, t * B_TILE + f + B_UP)

            def down(c, i, ready=None):
                j = c % 2
                for part in range(3):
                    a, b = DOWN_SPLIT[part], DOWN_SPLIT[part + 1]
                    if part == 2 and ready:
                        pe.wait_ge(*ready)
                    products(t, U_DOWN + 3 * c + part, i, bank[j][:, :], lambda k: g_hi[:, a + k, :],
                             lambda k: g_lo[:, a + k, :], b - a, first=part == 0, last=part == 2)

            pe.wait_ge(*up_dve.at("g_lo", t * KF + (KF - 2)))
            for c in range(KD):
                pe.wait_ge(evac[c % 2], t * B_TILE + (B_DOWN + c // 2))
                down(c, 0, up_dve.at("g_lo", t * KF + (KF - 1)) if c == 0 else None)
                if c == 3:
                    pe.wait_ge(*pre_dve.before((t + 1) * KD + KD))
                    token_sums(bank[6], sum_n).then_inc(*norm_pe.did("ssq"))
                if c == 4:
                    norm_spread(bank[7], diag_n, norm_dve, norm_pe, t + 1)
        pe.wait_ge(*res_dve.before(NT * KD))
        token_sums(bank[4], sum_r).then_inc(*fin_pe.did("ssq"))
        norm_spread(bank[5], diag_r, fin_dve, fin_pe, NT)

    block.__exit__(None, None, None)


_ORDER = ("x_t", "w_units", "par", "masks_in", "ident_in", "gm_wt", "ln_b", "gm_bs")


def _columns(a):
    import numpy as np
    return np.asarray(a).reshape(-1, P).T


def _units(inputs):
    import numpy as np

    def unit(w, col, k0=0, k1=None):
        a = np.asarray(w)[k0 * P:None if k1 is None else k1 * P, col * P:(col + 1) * P]
        return a.reshape(-1, P, P).transpose(1, 0, 2)

    w_in, w_up, w_down = inputs["w_in"][0], inputs["w_up"][0], inputs["w_down"][0]
    u_at, v_at, q_at, f_at, i_at, og_at = (NH * n for n in range(6))
    ga_at, gb_at = 6 * NH, 6 * NH + KD
    out = np.zeros((UNITS + 2, P, KD, P), np.float32)
    n = 0
    for at in (i_at, v_at):
        for k in range(0, KD, 2):
            out[n] = w_in[k * P:(k + 2) * P, at * P:(at + NH) * P].reshape(2, P, NH * P).transpose(1, 0, 2).reshape(P, KD, P)
            n += 1
    for h in range(NH):
        for col in (f_at + h, q_at + h, ga_at + h, og_at + h, gb_at + h, u_at + h):
            out[n] = unit(w_in, col)
            n += 1
    for p in range(KD // 2):
        out[n] = unit(w_in, ga_at + NH + p)
        out[n + 1] = unit(w_in, gb_at + NH + p)
        for j in range(2):
            c = 2 * p + j
            out[n + 2 + j, :, :NH] = unit(inputs["w_br_hg"][0], c)
            out[n + 2 + j, :, NH:] = unit(inputs["w_br_gm"][0], c)
        n += 4
    for c in range(KD):
        out[n] = unit(inputs["w_out"][0], c)
        n += 1
    for f in range(KF):
        out[n], out[n + 1] = unit(w_up, f), unit(w_up, KF + f)
        n += 2
    for c in range(KD):
        for a, b in zip(DOWN_SPLIT, DOWN_SPLIT[1:]):
            out[n, :, :b - a] = unit(w_down, c, a, b)
            n += 1
    out[n:] = out[:2]
    return out


def _masks():
    import numpy as np
    j = np.arange(P)[:, None]
    parts = [np.tile(j == np.arange(P)[None], (1, NC))]
    for s in LEVELS:
        i = np.arange(P // 2)[None]
        parts.append(np.tile((j // (2 * s) == i // s) & (j % (2 * s) < s), (1, NC)))
    return np.concatenate(parts, axis=1).astype(np.uint32)


def kernel(**inputs):
    import numpy as np
    import concourse.bacc as bacc
    from concourse.bass_utils import run_bass_kernel_spmd

    inputs = {k: np.asarray(v) for k, v in inputs.items()}
    x_t = np.zeros((NT + 1, P, KD, TT), np.float32)
    x_t[:NT] = inputs["x"][0].reshape(NT, TT, KD, P).transpose(0, 3, 2, 1)
    par = np.zeros((P, N_PAR), np.float32)
    for at, a in ((C_MIXN, inputs["mix_norm"][0]), (C_FFNN, inputs["ffn_norm"][0]), (C_FINN, inputs["final_norm"]),
                  (C_LB, inputs["hg_lb_logits"][0]), (C_LNG, inputs["gm_ln_g"][0]), (C_HGN, inputs["hg_norm_g"][0]),
                  (C_CW, inputs["conv_w"][0]), (C_CB, inputs["conv_b"][0])):
        cols = _columns(a)
        par[:, at:at + cols.shape[1]] = cols
    arrays = {
        "x_t": x_t,
        "w_units": _units(inputs),
        "par": par,
        "masks_in": _masks(),
        "ident_in": np.eye(P, dtype=np.float32),
        "gm_wt": np.ascontiguousarray(inputs["gm_ws"][0].transpose(2, 0, 1)),
        "ln_b": np.ascontiguousarray(inputs["gm_ln_b"][0:1]),
        "gm_bs": np.ascontiguousarray(inputs["gm_bs"][0].reshape(1, NH * P)),
    }
    nc = bacc.Bacc("TRN2", target_bir_lowering=False, num_devices=1)
    args = [nc.dram_tensor(n, arrays[n].shape, mybir.dt.from_np(arrays[n].dtype), kind="ExternalInput").ap()
            for n in _ORDER]
    out = nc.dram_tensor("out", (NT + 1, P, KD, TT), F32, kind="ExternalOutput").ap()
    build(nc, *args, out)
    r = run_bass_kernel_spmd(nc, [arrays], core_ids=[0])
    got = r.results[0]["out"][1:]
    return np.ascontiguousarray(got.transpose(0, 3, 2, 1).reshape(1, SEQ, D))
```
